# Optimizing a Trainium2 kernel written in Bass

```python
import jax, jax.numpy as jnp
from jax import lax
import numpy as np

D_MODEL = 1024
BATCH = 1
SEQ = 512
DEPTH = 2

HEAD_DIM = 64
N_HEADS = D_MODEL // HEAD_DIM
ATTN_DIM = N_HEADS * HEAD_DIM
D_FF = 256 * ((8 * D_MODEL // 3 + 255) // 256)
ROPE_THETA = 10000.0
RMS_EPS = 1e-6
N_A_LAYERS = DEPTH // 2
N_B_LAYERS = DEPTH - N_A_LAYERS
MOBA_BLOCK = 256
MOBA_TOPK = 3
MOBA_Q_CHUNK = 16
DILATED_BRANCHES = ((128, 1), (512, 4), (2048, 16))
N_BRANCHES = len(DILATED_BRANCHES)
N_SUBLAYERS = 3

kernel_name = "yoco_moba_longnet_macaron_adaln"

def rms_norm(x, g):
    x32 = x.astype(jnp.float32)
    y = x32 * lax.rsqrt(jnp.mean(x32 * x32, axis=-1, keepdims=True) + RMS_EPS)
    return (y * g.astype(jnp.float32)).astype(x.dtype)

def modulate(h, shift, scale):
    return h * (1 + scale[:, None, :]) + shift[:, None, :]

def rope_tables(seq_len):
    inv = 1.0 / (ROPE_THETA ** (jnp.arange(0, HEAD_DIM, 2, dtype=jnp.float32) / HEAD_DIM))
    ang = jnp.arange(seq_len, dtype=jnp.float32)[:, None] * inv[None, :]
    return jnp.cos(ang), jnp.sin(ang)

def apply_rope(x, cos, sin):
    x32 = x.astype(jnp.float32)
    x1, x2 = jnp.split(x32, 2, axis=-1)
    c = cos[None, :, None, :]
    s = sin[None, :, None, :]
    return jnp.concatenate([x1 * c - x2 * s, x2 * c + x1 * s], axis=-1).astype(x.dtype)

def swiglu(h, w_gate, w_up, w_down):
    return (jax.nn.silu(h @ w_gate) * (h @ w_up)) @ w_down

def moba_attention(q, k, v):
    B, S, H, Dh = q.shape
    nb = -(-S // MOBA_BLOCK)
    Sp = nb * MOBA_BLOCK
    pad = ((0, 0), (0, Sp - S), (0, 0), (0, 0))
    q, k, v = jnp.pad(q, pad), jnp.pad(k, pad), jnp.pad(v, pad)
    scale = Dh ** -0.5
    kb = k.reshape(B, nb, MOBA_BLOCK, H, Dh)
    vb = v.reshape(B, nb, MOBA_BLOCK, H, Dh)
    k_mean = jnp.mean(kb.astype(jnp.float32), axis=2)
    gate = jnp.einsum('bshd,bnhd->bshn', q.astype(jnp.float32), k_mean)
    q_block = jnp.arange(Sp) // MOBA_BLOCK
    past = jnp.arange(nb)[None, :] < q_block[:, None]
    gate = jnp.where(past[None, :, None, :], gate, -jnp.inf)
    n_sel = min(MOBA_TOPK, max(nb - 1, 1))
    top_val, top_idx = lax.top_k(gate, n_sel)
    sel_valid = top_val > -jnp.inf
    kb_t = kb.transpose(0, 3, 1, 2, 4)
    vb_t = vb.transpose(0, 3, 1, 2, 4)
    n_chunks = Sp // MOBA_Q_CHUNK

    def to_chunks(t):
        return t.reshape(B, n_chunks, MOBA_Q_CHUNK, *t.shape[2:]).swapaxes(0, 1)

    b_ix = jnp.arange(B)[:, None, None, None]
    h_ix = jnp.arange(H)[None, None, :, None]
    in_blk = jnp.arange(MOBA_BLOCK)

    def chunk_fn(args):
        start, qc, idx, valid = args
        blk = start // MOBA_BLOCK
        k_own = lax.dynamic_slice_in_dim(k, blk * MOBA_BLOCK, MOBA_BLOCK, axis=1)
        v_own = lax.dynamic_slice_in_dim(v, blk * MOBA_BLOCK, MOBA_BLOCK, axis=1)
        q_pos = start + jnp.arange(MOBA_Q_CHUNK)
        k_pos = blk * MOBA_BLOCK + in_blk
        s_own = jnp.einsum('bqhd,bkhd->bqhk', qc, k_own).astype(jnp.float32) * scale
        causal = (k_pos[None, :] <= q_pos[:, None])[None, :, None, :]
        s_own = jnp.where(causal, s_own, -jnp.inf)
        k_sel = kb_t[b_ix, h_ix, idx]
        v_sel = vb_t[b_ix, h_ix, idx]
        s_sel = jnp.einsum('bqhd,bqhnkd->bqhnk', qc, k_sel).astype(jnp.float32) * scale
        s_sel = jnp.where(valid[..., None], s_sel, -jnp.inf)
        s_sel = s_sel.reshape(B, MOBA_Q_CHUNK, H, n_sel * MOBA_BLOCK)
        p = jax.nn.softmax(jnp.concatenate([s_own, s_sel], axis=-1), axis=-1).astype(v.dtype)
        p_own = p[..., :MOBA_BLOCK]
        p_sel = p[..., MOBA_BLOCK:].reshape(B, MOBA_Q_CHUNK, H, n_sel, MOBA_BLOCK)
        return (jnp.einsum('bqhk,bkhd->bqhd', p_own, v_own)
                + jnp.einsum('bqhnk,bqhnkd->bqhd', p_sel, v_sel))

    starts = jnp.arange(n_chunks, dtype=jnp.int32) * MOBA_Q_CHUNK
    out = lax.map(chunk_fn, (starts, to_chunks(q), to_chunks(top_idx), to_chunks(sel_valid)))
    out = out.swapaxes(0, 1).reshape(B, Sp, H, Dh)
    return out[:, :S]

def moba_mixer(h, w_qkv, w_o, cos, sin):
    B, S, _ = h.shape
    qkv = (h @ w_qkv).reshape(B, S, 3, N_HEADS, HEAD_DIM)
    q = apply_rope(qkv[:, :, 0], cos, sin)
    k = apply_rope(qkv[:, :, 1], cos, sin)
    v = qkv[:, :, 2]
    return moba_attention(q, k, v).reshape(B, S, ATTN_DIM) @ w_o

def to_strided(x, d):
    B, S = x.shape[:2]
    return x.reshape(B, S // d, d, *x.shape[2:]).swapaxes(1, 2).reshape(B * d, S // d, *x.shape[2:])

def from_strided(x, d, B):
    L = x.shape[1]
    return x.reshape(B, d, L, *x.shape[2:]).swapaxes(1, 2).reshape(B, L * d, *x.shape[2:])

def band_kv(t, n_dist):
    N, L = t.shape[:2]
    nb = -(-L // n_dist)
    tp = jnp.pad(t, ((0, 0), (n_dist, nb * n_dist - L), (0, 0), (0, 0)))
    tb = tp.reshape(N, nb + 1, n_dist, *t.shape[2:])
    return jnp.concatenate([tb[:, :-1], tb[:, 1:]], axis=2)

def band_attention(q, k_band, v_band, n_dist):
    N, L, H, Dh = q.shape
    nb = k_band.shape[1]
    qb = jnp.pad(q, ((0, 0), (0, nb * n_dist - L), (0, 0), (0, 0))).reshape(N, nb, n_dist, H, Dh)
    s = jnp.einsum('nbqhd,nbkhd->nbhqk', qb, k_band).astype(jnp.float32) * (Dh ** -0.5)
    a = jnp.arange(n_dist)[:, None]
    j = jnp.arange(2 * n_dist)[None, :]
    blk = jnp.arange(nb)[:, None, None]
    allowed = (j >= a) & (j <= a + n_dist) & (blk * n_dist + j >= n_dist)
    s = jnp.where(allowed[None, :, None], s, -jnp.inf)
    m = jnp.max(s, axis=-1, keepdims=True)
    p = jnp.exp(s - m)
    l = jnp.sum(p, axis=-1, keepdims=True)
    o = jnp.einsum('nbhqk,nbkhd->nbqhd', (p / l).astype(v_band.dtype), v_band)
    lse = (m + jnp.log(l))[..., 0]
    o = o.reshape(N, nb * n_dist, H, Dh)[:, :L]
    lse = lse.transpose(0, 1, 3, 2).reshape(N, nb * n_dist, H)[:, :L]
    return o, lse

def shared_kv_bands(h, w_kv, cos, sin):
    B, S, _ = h.shape
    kv = (h @ w_kv).reshape(B, S, N_BRANCHES, 2, N_HEADS, HEAD_DIM)
    bands = []
    for g, (window, dil) in enumerate(DILATED_BRANCHES):
        n_dist = window // dil
        k = apply_rope(kv[:, :, g, 0], cos, sin)
        v = kv[:, :, g, 1]
        bands.append((band_kv(to_strided(k, dil), n_dist), band_kv(to_strided(v, dil), n_dist)))
    return bands

def dilated_mixer(h, w_q, w_o, kv_bands, cos, sin):
    B, S, _ = h.shape
    q = apply_rope((h @ w_q).reshape(B, S, N_BRANCHES * N_HEADS, HEAD_DIM), cos, sin)
    q = q.reshape(B, S, N_BRANCHES, N_HEADS, HEAD_DIM)
    outs, lses = [], []
    for g, (window, dil) in enumerate(DILATED_BRANCHES):
        k_band, v_band = kv_bands[g]
        o, lse = band_attention(to_strided(q[:, :, g], dil), k_band, v_band, window // dil)
        outs.append(from_strided(o, dil, B))
        lses.append(from_strided(lse, dil, B))
    w = jax.nn.softmax(jnp.stack(lses, axis=0), axis=0).astype(h.dtype)
    o = jnp.einsum('gbsh,gbshd->bshd', w, jnp.stack(outs, axis=0))
    return o.reshape(B, S, ATTN_DIM) @ w_o

def setup_inputs(seed: int = 0) -> dict:
    key = jax.random.key(seed)
    ks = jax.random.split(key, 17)
    D, F = D_MODEL, D_FF

    def w(k, shape, fan_in, gain=1.0):
        return jax.random.normal(k, shape, jnp.float32) * (gain * fan_in ** -0.5)

    def norm_gain(k, shape):
        return 1.0 + 0.05 * jax.random.normal(k, shape, jnp.float32)

    return {
        "x": jax.random.normal(ks[0], (BATCH, SEQ, D), jnp.float32),
        "c": jax.random.normal(ks[1], (BATCH, D), jnp.float32),
        "ada_w": w(ks[2], (DEPTH, D, N_SUBLAYERS * 3 * D), D, 0.5),
        "ada_b": 0.02 * jax.random.normal(ks[3], (DEPTH, N_SUBLAYERS * 3 * D), jnp.float32),
        "norm_g": norm_gain(ks[4], (DEPTH, N_SUBLAYERS, D)),
        "ffn_w_gate": w(ks[5], (DEPTH, 2, D, F), D),
        "ffn_w_up": w(ks[6], (DEPTH, 2, D, F), D),
        "ffn_w_down": w(ks[7], (DEPTH, 2, F, D), F),
        "moba_w_qkv": w(ks[8], (N_A_LAYERS, D, 3 * ATTN_DIM), D),
        "moba_w_o": w(ks[9], (N_A_LAYERS, ATTN_DIM, D), ATTN_DIM),
        "kv_ada_w": w(ks[10], (D, 2 * D), D, 0.5),
        "kv_ada_b": 0.02 * jax.random.normal(ks[11], (2 * D,), jnp.float32),
        "kv_norm_g": norm_gain(ks[12], (D,)),
        "kv_w": w(ks[13], (D, N_BRANCHES * 2 * ATTN_DIM), D),
        "dil_w_q": w(ks[14], (N_B_LAYERS, D, N_BRANCHES * ATTN_DIM), D),
        "dil_w_o": w(ks[15], (N_B_LAYERS, ATTN_DIM, D), ATTN_DIM),
        "final_g": norm_gain(ks[16], (D,)),
    }

def reference(x, c, ada_w, ada_b, norm_g, ffn_w_gate, ffn_w_up, ffn_w_down,
              moba_w_qkv, moba_w_o, kv_ada_w, kv_ada_b, kv_norm_g, kv_w,
              dil_w_q, dil_w_o, final_g):
    B, S, D = x.shape
    cos, sin = rope_tables(S)
    c_act = jax.nn.silu(c)
    kv_bands = None
    for layer in range(DEPTH):
        if layer == N_A_LAYERS:
            kv_mod = (c_act @ kv_ada_w + kv_ada_b).reshape(B, 2, D)
            h_kv = modulate(rms_norm(x, kv_norm_g), kv_mod[:, 0], kv_mod[:, 1])
            kv_bands = shared_kv_bands(h_kv, kv_w, cos, sin)
        mod = (c_act @ ada_w[layer] + ada_b[layer]).reshape(B, N_SUBLAYERS, 3, D)
        h = modulate(rms_norm(x, norm_g[layer, 0]), mod[:, 0, 0], mod[:, 0, 1])
        x = x + 0.5 * mod[:, 0, 2][:, None, :] * swiglu(h, ffn_w_gate[layer, 0], ffn_w_up[layer, 0], ffn_w_down[layer, 0])
        h = modulate(rms_norm(x, norm_g[layer, 1]), mod[:, 1, 0], mod[:, 1, 1])
        if layer < N_A_LAYERS:
            y = moba_mixer(h, moba_w_qkv[layer], moba_w_o[layer], cos, sin)
        else:
            lb = layer - N_A_LAYERS
            y = dilated_mixer(h, dil_w_q[lb], dil_w_o[lb], kv_bands, cos, sin)
        x = x + mod[:, 1, 2][:, None, :] * y
        h = modulate(rms_norm(x, norm_g[layer, 2]), mod[:, 2, 0], mod[:, 2, 1])
        x = x + 0.5 * mod[:, 2, 2][:, None, :] * swiglu(h, ffn_w_gate[layer, 1], ffn_w_up[layer, 1], ffn_w_down[layer, 1])
    return rms_norm(x, final_g)


_drawn_inputs = setup_inputs


def setup_inputs(seed=0):
    import zlib

    import numpy as np

    out = dict(_drawn_inputs(seed))
    spreads = {}
    factors = {'ada_b': 2.789, 'norm_g': 3.48, 'kv_ada_b': 8.0, 'kv_norm_g': 8.0}
    for name, (base, spread) in spreads.items():
        noise = np.random.default_rng([zlib.crc32(name.encode()), seed]).standard_normal(out[name].shape)
        drawn = base * np.exp(spread * noise) if base else spread * noise
        out[name] = __import__('jax').numpy.asarray(drawn.astype(out[name].dtype))
    for name, factor in factors.items():
        out[name] = (out[name] * factor).astype(out[name].dtype)
    return out
```

```python
from contextlib import ExitStack

import numpy as np

import concourse.bass as bass
from concourse import mybir

F32 = mybir.dt.float32
F32R = mybir.dt.float32r
BF16 = mybir.dt.bfloat16
ALU = mybir.AluOpType
ACT = mybir.ActivationFunctionType

P = 128
D = 1024
S = 512
F = 2816
HEADS = 16
HD = 64
EPS = 1e-6
KT = D // P
FT = F // P
TT = S // P
G = HEADS // 4
HALF = HD // 2
NB = 3
UNIT = 1024
PAIR = 256
DOWN_KS = (4, 4, 4, 4, 4, 2)
FULL_KS = (4, 4)
ADA_W = 1024
MASKED = -1e30
FAR = 3e38

FFN_UNITS = 2 * FT + 4 * len(DOWN_KS)
PHASES = (("ffn0", FFN_UNITS), ("mixA", 24), ("woA", 8), ("ffn1", FFN_UNITS), ("kv", 48),
          ("ffn2", FFN_UNITS), ("mixB", 24), ("woB", 8), ("ffn3", FFN_UNITS))
UNIT0, PAIR0 = {}, {}
_u = _p = 0
for _name, _n in PHASES:
    UNIT0[_name], PAIR0[_name] = _u, _p
    _u += _n
    _p += FT + 4 if _name[:3] == "ffn" else _n // 2
UNITS = _u
ADA_IN_FFN = {0: (2, 6), 1: (8, 6), 2: (14, 6), 3: (20, 0)}
ADA_SLOTS = 4
SUB_BLOCK = (0, 3, 6, 11, 14, 17)
KV_BLOCK = 9
ADA_BLOCKS = 20
GAIN_KV, GAIN_FINAL = 6, 7
ROUND = {"ffn0": 0, "mixA": 1, "ffn1": 2, "kv": 3, "mixB": 4, "ffn3": 5, "final": 6}

PRE, STEPS = 8, 16
IN_STEPS = 12


def build(nc, x_t, c_col, ada, ada_bias, gains, gate_up, down, mixa_w, kv_w, mixb_w, cos_t, sin_t,
          mask_a, mask_b, ident_in, out):
    with ExitStack() as ctx:
        def sem(name):
            return ctx.enter_context(nc.semaphore(name))

        def sb(stack, name, shape, dt=F32):
            return stack.enter_context(nc.sbuf_tensor(name, shape, dt))

        x = sb(ctx, "x", [P, KT, S])
        h_hi = sb(ctx, "h_hi", [P, KT, S], F32R)
        h_lo = sb(ctx, "h_lo", [P, KT, S], F32R)
        w_raw = sb(ctx, "w_raw", [P, 2, UNIT])
        w_hi = sb(ctx, "w_hi", [P, 2, UNIT], F32R)
        w_lo = sb(ctx, "w_lo", [P, 2, UNIT], F32R)
        tmp = sb(ctx, "tmp", [P, 5, S])
        diag = sb(ctx, "diag", [P, TT, P])
        ident = sb(ctx, "ident", [P, P])
        ones = sb(ctx, "ones", [P, P])
        mod = sb(ctx, "mod", [P, ADA_BLOCKS, KT])
        mod_bias = sb(ctx, "mod_bias", [P, ADA_BLOCKS, KT])
        gain = sb(ctx, "gain", [P, 8, KT])
        c_in = sb(ctx, "c_in", [P, KT])
        c_act = sb(ctx, "c_act", [P, KT])
        mod_sum = sb(ctx, "mod_sum", [P, KT])
        a_col = sb(ctx, "a_col", [P, KT])
        g_col = sb(ctx, "g_col", [P, KT])
        rms = sb(ctx, "rms", [P, TT])
        rinv = sb(ctx, "rinv", [P, TT])
        eps = sb(ctx, "eps", [P, 1])
        with ExitStack() as ffn_space:
            act_hi = sb(ffn_space, "act_hi", [P, FT, S], F32R)
            act_lo = sb(ffn_space, "act_lo", [P, FT, S], F32R)
            silu_g = sb(ffn_space, "silu_g", [P, 2, S])
            prod = sb(ffn_space, "prod", [P, 2, S])
            ada_raw = sb(ffn_space, "ada_raw", [P, ADA_SLOTS, ADA_W])
            ada_acc = sb(ffn_space, "ada_acc", [P, ADA_W])
        with ExitStack() as mixer_space:
            cos = sb(mixer_space, "cos", [P, S])
            sin = sb(mixer_space, "sin", [P, S])
            rotated = sb(mixer_space, "rotated", [P, 2, S])
            v_out = sb(mixer_space, "v_out", [P, 4, TT, HD])
            q_raw = sb(mixer_space, "q_raw", [P, NB, S])
            k_raw = sb(mixer_space, "k_raw", [P, NB, S])
            v_raw = sb(mixer_space, "v_raw", [P, NB, TT, HD])
            q_st = sb(mixer_space, "q_st", [P, 2, NB, S], F32R)
            k_hi = sb(mixer_space, "k_hi", [P, 2, NB, S], F32R)
            k_lo = sb(mixer_space, "k_lo", [P, 2, NB, S], F32R)
            v_hi = sb(mixer_space, "v_hi", [P, 2, NB, TT, HD], F32R)
            v_lo = sb(mixer_space, "v_lo", [P, 2, NB, TT, HD], F32R)
            probs = sb(mixer_space, "probs", [P, 2, 6 * P])
            pt_hi = sb(mixer_space, "pt_hi", [P, 6 * P], F32R)
            pt_lo = sb(mixer_space, "pt_lo", [P, 6 * P], F32R)
            o_rows = sb(mixer_space, "o_rows", [P, TT, 4 * HD])
            att = sb(mixer_space, "att", [P, KT, S])
            m_a = sb(mixer_space, "m_a", [P, TT * P], BF16)
            m_b = sb(mixer_space, "m_b", [P, TT, 6 * P], BF16)
            negmax = sb(mixer_space, "negmax", [P, 2])
            denom = sb(mixer_space, "denom", [P, 4])
            rdenom = sb(mixer_space, "rdenom", [P, 2])

        ps = ctx.enter_context(nc.psum_tensor("ps", [P, 8, 512], F32))
        flat = ps[:].rearrange("p b n -> p (b n)")
        rb = ps[:, 4, :]
        stat = ps[:, 5, 0:TT]
        ada_ps = flat[:, 6 * 512:6 * 512 + ADA_W]
        scores = flat[:, 4 * 512:4 * 512 + 6 * P]
        pt_ps = flat[:, 6 * 512:6 * 512 + 6 * P]
        o_ps = ps[:, 5, 256:256 + HD]
        ot_ps = ps[:, 6, :]

        def scratch(name, shape):
            return nc.dram_tensor(name, shape, F32, kind="Internal").ap()

        dram_q = {"A": scratch("qa", (G, 1, 2, P, S)), "B": scratch("qb", (G, NB, 2, P, S))}
        dram_k = {"A": scratch("ka", (G, 1, 2, P, S)), "B": scratch("kb", (G, NB, 2, P, S))}
        dram_v = {"A": scratch("va", (G, 1, 4, P, TT * HD)), "B": scratch("vb", (G, NB, 4, P, TT * HD))}

        w_landed = [sem("w_landed0"), sem("w_landed1")]
        w_hi_done = sem("w_hi_done")
        w_lo_done = [sem("w_lo_done0"), sem("w_lo_done1")]
        unit_used = sem("unit_used")
        pair_free = sem("pair_free")
        consts_in, x_in, tables_in = sem("consts_in"), sem("x_in"), sem("tables_in")
        c_ready, setup = sem("c_ready"), sem("setup")
        ada_landed = [sem(f"ada_landed{n}") for n in range(ADA_SLOTS)]
        ada_added = sem("ada_added")
        ada_summed = sem("ada_summed")
        lanes_summed = sem("lanes_summed")
        mod_ready = sem("mod_ready")
        col_ready = sem("col_ready")
        silu_done, act_hi_done, act_lo_done = sem("silu_done"), sem("act_hi_done"), sem("act_lo_done")
        x_first = sem("x_first")
        sq_done, sum_done = sem("sq_done"), sem("sum_done")
        stat_done, rms_done, rinv_done = sem("stat_done"), sem("rms_done"), sem("rinv_done")
        diag_done, rb_done = sem("diag_done"), sem("rb_done")
        xar_done, h_hi_done, h_lo_done = sem("xar_done"), sem("h_hi_done"), sem("h_lo_done")
        rope_done = sem("rope_done")
        v_out_done = sem("v_out_done")
        q_stored, k_stored, v_stored = sem("q_stored"), sem("k_stored"), sem("v_stored")
        q_landed, k_landed, v_landed = sem("q_landed"), sem("k_landed"), sem("v_landed")
        prep_hi, prep_lo = sem("prep_hi"), sem("prep_lo")
        s_done, negmax_done, exp_done = sem("s_done"), sem("negmax_done"), sem("exp_done")
        t_done, pt_hi_done, pt_lo_done = sem("t_done"), sem("pt_hi_done"), sem("pt_lo_done")
        pv_done, rd_done, o_done = sem("pv_done"), sem("rd_done"), sem("o_done")
        ot_done = sem("ot_done")
        att_done = sem("att_done")
        y_done, out_stored = sem("y_done"), sem("out_stored")
        carrier = sem("carrier")

        def classes(ap):
            return ap.rearrange("p (c l) -> p c l", c=4)

        def by_class(ap):
            return ap.rearrange("p (l c) -> p c l", c=4)


        def h_count(name):
            order = ("ffn0", "mixA", "woA", "ffn1", "kv", "ffn2", "mixB", "woB", "ffn3")
            return KT * order.index(name)

        def rope_before(name):
            return {"mixA": 0, "kv": 16, "mixB": 40}[name]

        def w_dma(sp, u, slot, src, first=False):
            if not first:
                sp.wait_ge(w_lo_done[slot], u - slot)
            n = src.shape[1]
            sp.dma_start(w_raw[:, slot, 0:n], src).then_inc(w_landed[slot], 16)

        def w_split_hi(act, u, slot, n=UNIT, first=False):
            act.wait_ge(w_landed[slot], u * 8 - slot * 8 + 16)
            if not first:
                act.wait_ge(unit_used, u - 1)
            nc.scalar.copy(w_hi[:, slot, 0:n], w_raw[:, slot, 0:n]).then_inc(w_hi_done, 1)

        def w_split_lo(eng, u, slot, n=UNIT):
            eng.wait_ge(w_hi_done, u + 1)
            eng.tensor_tensor(w_lo[:, slot, 0:n], w_raw[:, slot, 0:n],
                              w_hi[:, slot, 0:n].bitcast(F32), ALU.subtract).then_inc(w_lo_done[slot], 2)

        def three_passes(out_ap, l_hi, l_lo, r_hi, r_lo, start, stop, skip=False):
            nc.tensor.matmul(out_ap, l_hi, r_hi, start=start, stop=False, skip_group_check=skip)
            nc.tensor.matmul(out_ap, l_hi, r_lo, start=False, stop=False, skip_group_check=skip)
            return nc.tensor.matmul(out_ap, l_lo, r_hi, start=False, stop=stop, skip_group_check=skip)

        def pe_k_tile(bank, slot, k4, in_hi, in_lo, k, last_k):
            for j in range(2):
                cols = slice(k4 * PAIR + j * P, k4 * PAIR + (j + 1) * P)
                mm = three_passes(ps[:, bank + j, :], w_hi[:, slot, cols], w_lo[:, slot, cols],
                                  in_hi[:, k, :], in_lo[:, k, :], k == 0, k == last_k)
            return mm

        def pe_k_tile_v(bank, slot, k4, k, last_k):
            cols = slice(k4 * PAIR, (k4 + 1) * PAIR)
            for t in range(TT):
                o = ps[:, bank + t // 2, (t % 2) * PAIR:(t % 2 + 1) * PAIR]
                tokens = slice(t * P, (t + 1) * P)
                mm = three_passes(o, h_hi[:, k, tokens], h_lo[:, k, tokens],
                                  w_hi[:, slot, cols], w_lo[:, slot, cols],
                                  k == 0 and t % 2 == 0, k == last_k, skip=True)
            return mm

        def pe_stats(pe, r):
            pe.wait_ge(sum_done, 9 * (r + 1))
            for t in range(TT):
                mm = nc.tensor.matmul(stat[:, t:t + 1], tmp[:, 2, t * P:(t + 1) * P], ones[:, 0:1],
                                      start=True, stop=True)
            mm.then_inc(stat_done, 1)
            pe.wait_ge(diag_done, r + 1)
            nc.tensor.matmul(rb, ones[:], diag[:].rearrange("p t n -> p (t n)"),
                             start=True, stop=True).then_inc(rb_done, 1)

        def pe_ada_sum(pe, block):
            pe.wait_ge(ada_added, block * KT + KT)
            pe.wait_ge(mod_ready, block)
            for n in range(KT):
                cols = slice(n * P, (n + 1) * P)
                mm = nc.tensor.transpose(ada_ps[:, cols], ada_acc[:, cols], ident[:])
            mm.then_inc(ada_summed, 1)

        def pe_pair(pe, u0, pair, bank, ks, in_hi, in_lo, k_ready=None, between=None):
            last_k, k = sum(ks) - 1, 0
            for j, kn in enumerate(ks):
                pe.wait_ge(w_lo_done[j % 2], u0 + j - j % 2 + 2)
                if j == 0:
                    pe.wait_ge(pair_free, pair + 1)
                for k4 in range(kn):
                    if k_ready is not None:
                        k_ready(pe, k)
                    mm = pe_k_tile(bank, j % 2, k4, in_hi, in_lo, k, last_k)
                    k += 1
                mm.then_inc(unit_used, 1)
                if j == 0 and between is not None:
                    between()

        def pe_ffn(pe, f):
            name = f"ffn{f}"
            u0, p0, h0 = UNIT0[name], PAIR0[name], h_count(name)
            block0, blocks = ADA_IN_FFN[f]

            def h_ready(pe, k):
                pe.wait_ge(h_lo_done, h0 + k + 1)

            def body(i, ada_before):
                for b in range(2):
                    between = (lambda: pe_ada_sum(pe, i + block0 - 1)) if ada_before and b == 0 else None
                    pe_pair(pe, i * 4 + u0 + 2 * b, i * 2 + p0 + b, 2 * b, FULL_KS, h_hi, h_lo,
                            h_ready if b == 0 else None, between)

            body(0, False)
            if blocks:
                with pe.Fori(1, blocks + 1) as i:
                    body(i, True)
            with pe.Fori(blocks + 1, FT // 2) as i:
                body(i, False)

            def act_ready(pe, k):
                if k in (0, FT - 2, FT - 1):
                    pe.wait_ge(act_lo_done, FT * f + max(k + 1, FT - 2))
            pe_residual(pe, u0 + 2 * FT, p0 + FT, DOWN_KS, act_hi, act_lo, act_ready)

        def pe_residual(pe, u0, p0, ks, in_hi, in_lo, ready):
            with pe.Fori(0, 2) as i:
                for b in range(2):
                    pe_pair(pe, i * (2 * len(ks)) + u0 + len(ks) * b, i * 2 + p0 + b, 2 * b, ks,
                            in_hi, in_lo, ready if b == 0 else None)

        def pe_wo(pe, name):
            h0 = h_count(name)

            def h_ready(pe, k):
                pe.wait_ge(h_lo_done, h0 + k + 1)
            pe_residual(pe, UNIT0[name], PAIR0[name], FULL_KS, h_hi, h_lo, h_ready)

        def pe_kv(pe):
            u0, p0, h0 = UNIT0["kv"], PAIR0["kv"], h_count("kv")

            def h_ready(pe, k):
                pe.wait_ge(h_lo_done, h0 + k + 1)

            with pe.Fori(0, G * NB) as i:
                pe_pair(pe, i * 4 + u0, i * 2 + p0, 0, FULL_KS, h_hi, h_lo, h_ready)
                for j in range(2):
                    pe.wait_ge(w_lo_done[j], i * 4 + u0 + 2 + 2)
                    if j == 0:
                        pe.wait_ge(pair_free, i * 2 + p0 + 2)
                    for k4 in range(4):
                        mm = pe_k_tile_v(2, j, k4, 4 * j + k4, KT - 1)
                    mm.then_inc(unit_used, 1)

        def pe_mixer(pe, name):
            layer = name[-1]
            is_a = layer == "A"
            nb = 1 if is_a else NB
            u0, p0, h0 = UNIT0[name], PAIR0[name], h_count(name)
            st0, hd0 = (0, 0) if is_a else (STEPS * G, HEADS)

            def tiles(s):
                return s % 4 + 1 if is_a else 6

            def substep(g, n):
                pair, k = n // KT, n % KT
                unit, bank = n // 4, 2 * (pair % 2)
                if n % 4 == 0:
                    pe.wait_ge(w_lo_done[unit % 2], g * 6 + u0 + unit - unit % 2 + 2)
                if k == 0:
                    pe.wait_ge(pair_free, g * 3 + p0 + pair + (2 if pair == 0 else 1))
                if n < KT:
                    pe.wait_ge(h_lo_done, h0 + k + 1)
                if is_a and pair == 2:
                    mm = pe_k_tile_v(bank, unit % 2, k % 4, k, KT - 1)
                else:
                    mm = pe_k_tile(bank, unit % 2, k % 4, h_hi, h_lo, k, KT - 1)
                if n % 4 == 3:
                    mm.then_inc(unit_used, 1)

            def score(a, s):
                sl, i = (s // 4) % 2, s % 4
                if i == 0:
                    pe.wait_ge(prep_lo, a * 12 + 3 * (hd0 + s // 4) + 2)
                if s >= 1:
                    pe.wait_ge(negmax_done, a * STEPS + st0 + s)
                if not is_a and s >= 3:
                    pe.wait_ge(o_done, a * STEPS + st0 + s - 2)
                tile, past = slice(i * P, (i + 1) * P), slice(0, (i + 1) * P)
                if is_a:
                    qs = [q_st[:, sl, 0, tile]]
                    keys = [(k_hi[:, sl, 0, past], k_lo[:, sl, 0, past], scores[:, past])]
                else:
                    keys = [(k_hi[:, sl, 0, :], k_lo[:, sl, 0, :], scores[:, 0:4 * P])]
                    for b in (1, 2):
                        keys.append((k_hi[:, sl, b, tile], k_lo[:, sl, b, tile],
                                     scores[:, (3 + b) * P:(4 + b) * P]))
                    qs = [q_st[:, sl, b, tile] for b in range(NB)]
                for q, (kh, kl, o) in zip(qs, keys):
                    nc.tensor.matmul(o, q, kh, start=True, stop=False)
                    mm = nc.tensor.matmul(o, q, kl, start=False, stop=True)
                mm.then_inc(s_done, 1)

            def transpose_p(a, s):
                st = a * STEPS + st0 + s
                pe.wait_ge(exp_done, st + 1)
                if s >= 1:
                    pe.wait_ge(pt_lo_done, st)
                if s in (0, 10):
                    pe.wait_ge(att_done, a * 2 + 2 * (st0 // STEPS) + (1 if s == 0 else 2))
                for n in range(tiles(s)):
                    mm = nc.tensor.transpose(pt_ps[:, n * P:(n + 1) * P], probs[:, s % 2, n * P:(n + 1) * P],
                                             ident[:])
                mm.then_inc(t_done, 1)

            def weigh_v(a, s):
                sl = (s // 4) % 2
                pe.wait_ge(pt_lo_done, a * STEPS + st0 + s + 1)
                if s % 4 == 0:
                    pe.wait_ge(prep_lo, a * 12 + 3 * (hd0 + s // 4) + 3)
                if s >= 1:
                    pe.wait_ge(o_done, a * STEPS + st0 + s)
                if not is_a:
                    pe.wait_ge(negmax_done, a * STEPS + st0 + min(s + 3, STEPS))
                n_last = tiles(s) - 1
                for n in range(tiles(s)):
                    b, t = (0, n) if n < 4 else (n - 3, s % 4)
                    cols = slice(n * P, (n + 1) * P)
                    mm = three_passes(o_ps, pt_hi[:, cols], pt_lo[:, cols], v_hi[:, sl, b, t, :],
                                      v_lo[:, sl, b, t, :], n == 0, n == n_last)
                mm.then_inc(pv_done, 1)

            def transpose_o(a, hp):
                pe.wait_ge(o_done, a * STEPS + st0 + 8 * hp + 8)
                pe.wait_ge(pt_lo_done, a * STEPS + st0 + (10 if hp == 0 else 16))
                for t in range(TT):
                    mm = nc.tensor.transpose(ot_ps[:, t * P:(t + 1) * P], o_rows[:, t, hp * P:(hp + 1) * P], ident[:])
                mm.then_inc(ot_done, 1)

            def group(g, gemm, attend):
                a = None if g is None else g - 1
                if g is None:
                    a = G - 1
                if gemm:
                    for n in range(PRE):
                        substep(g, n)
                if not attend:
                    for n in range(PRE, 24):
                        substep(g, n)
                    return
                for s in range(STEPS):
                    score(a, s)
                    if gemm and s < IN_STEPS:
                        substep(g, PRE + s)
                    if s >= 2:
                        weigh_v(a, s - 2)
                    if s == 11:
                        transpose_o(a, 0)
                    if s >= 1:
                        transpose_p(a, s - 1)
                if gemm:
                    substep(g, 20)
                weigh_v(a, 14)
                if gemm:
                    substep(g, 21)
                transpose_p(a, 15)
                if gemm:
                    substep(g, 22)
                    substep(g, 23)
                weigh_v(a, 15)
                transpose_o(a, 1)

            group(0, True, False)
            with pe.Fori(1, G) as g:
                group(g, True, True)
            group(None, False, True)


        def ada_dma(sp, block, k, first=False):
            v, slot = block * KT + k, k % ADA_SLOTS
            if not first:
                sp.wait_ge(ada_added, v - ADA_SLOTS + 1)
            sp.dma_start(ada_raw[:, slot, :], ada[block, k]).then_inc(ada_landed[slot], 16)

        def ada_add(dve, block, k):
            v, slot = block * KT + k, k % ADA_SLOTS
            turn = k // ADA_SLOTS
            dve.wait_ge(ada_landed[slot], block * (16 * KT // ADA_SLOTS) + 16 * turn + 16)
            if k == 0:
                dve.wait_ge(ada_summed, block)
                nc.vector.tensor_scalar(ada_acc[:], ada_raw[:, slot, :], c_act[:, 0:1], None,
                                        ALU.mult).then_inc(ada_added, 1)
            else:
                dve.wait_ge(ada_added, v)
                nc.vector.scalar_tensor_tensor(out=ada_acc[:], in0=ada_raw[:, slot, :],
                                               scalar=c_act[:, k:k + 1], in1=ada_acc[:],
                                               op0=ALU.mult, op1=ALU.add).then_inc(ada_added, 1)

        def mod_store(dve, block):
            dve.wait_ge(ada_summed, block + 1)
            nc.vector.tensor_reduce(mod_sum[:], ada_ps.rearrange("p (n l) -> p n l", n=KT),
                                    mybir.AxisListType.X, ALU.add).then_inc(lanes_summed, 1)
            dve.wait_ge(lanes_summed, block + 1)
            at = slice(block, block + 1) if isinstance(block, int) else bass.ds(block, 1)
            nc.vector.tensor_tensor(mod[:, at, :], mod_sum[:].rearrange("p (o n) -> p o n", o=1),
                                    mod_bias[:, at, :], ALU.add).then_inc(mod_ready, 1)

        NORMS = ("ffn0", "mixA", "ffn1", "kv", "ffn2", "mixB", "ffn3")

        def sum_clear(dve, r):
            dve.wait_ge(stat_done, r)
            nc.vector.memset(tmp[:, 2, :], 0.0).then_inc(sum_done, 1)

        def act_rms(act, r):
            act.wait_ge(stat_done, r + 1)
            nc.scalar.activation(rms[:], stat, ACT.Sqrt, bias=eps[:, 0:1], scale=1.0 / D).then_inc(rms_done, 1)

        def dve_diag(dve, r):
            dve.wait_ge(rms_done, r + 1)
            nc.vector.reciprocal(rinv[:], rms[:]).then_inc(rinv_done, 1)
            dve.wait_ge(rinv_done, r + 1)
            for t in range(TT):
                op = nc.vector.tensor_scalar(diag[:, t, :], ident[:], rinv[:, t:t + 1], None, ALU.mult)
            op.then_inc(diag_done, 1)

        def dve_norm(dve, name, r, block, gain_row, col_n):
            h0, view = h_count(name), by_class if name == "mixA" else classes
            dve.wait_ge(mod_ready, block + 2)
            nc.vector.scalar_tensor_tensor(out=a_col[:], in0=mod[:, block + 1, :], scalar=1.0,
                                           in1=gain[:, gain_row, :], op0=ALU.add,
                                           op1=ALU.mult).then_inc(col_ready, 1)
            dve.wait_ge(col_ready, col_n)
            dve.wait_ge(rb_done, r + 1)
            dve.wait_ge(unit_used, UNIT0[name])
            if name == "ffn2":
                dve.wait_ge(rope_done, rope_before("mixB"))

            def low(k):
                dve.wait_ge(h_hi_done, h0 + k + 1)
                nc.vector.scalar_tensor_tensor(out=view(h_lo[:, k, :]), in0=classes(tmp[:, 3 + k % 2, :]),
                                               scalar=mod[:, block, k:k + 1],
                                               in1=view(h_hi[:, k, :].bitcast(F32)), op0=ALU.add,
                                               op1=ALU.subtract).then_inc(h_lo_done, 1)
            for k in range(KT):
                if k >= 2:
                    dve.wait_ge(h_lo_done, h0 + k - 1)
                nc.vector.scalar_tensor_tensor(out=tmp[:, 3 + k % 2, :], in0=x[:, k, :],
                                               scalar=a_col[:, k:k + 1], in1=rb, op0=ALU.mult,
                                               op1=ALU.mult).then_inc(xar_done, 1)
                if k >= 1:
                    low(k - 1)
            low(KT - 1)

        def act_norm(act, name, block):
            x0, view = KT * NORMS.index(name), by_class if name == "mixA" else classes
            for k in range(KT):
                act.wait_ge(xar_done, x0 + k + 1)
                nc.scalar.activation(view(h_hi[:, k, :]), classes(tmp[:, 3 + k % 2, :]), ACT.Identity,
                                     bias=mod[:, block, k:k + 1]).then_inc(h_hi_done, 1)

        def split_sizes(ks, j):
            return ks[(j + 2) % len(ks)] * PAIR

        def act_residual(act, name, u0, p0, ks, r, res):
            n_u = len(ks)

            def body(i, last):
                for b in range(2):
                    u, p = i * (2 * n_u) + u0 + n_u * b, i * 2 + p0 + b
                    stop = last and b == 1
                    for j in range(n_u - 2 if stop else n_u - 1):
                        w_split_hi(act, u + j + 2, j % 2, split_sizes(ks, j))
                    for j in range(2):
                        n = i * 4 + 2 * b + j
                        if j == 0:
                            act.wait_ge(x_first, i * 2 + 4 * res + b + 1)
                        else:
                            act.wait_ge(pair_free, p + 3)
                        act.wait_ge(sum_done, n + 9 * r)
                        nc.scalar.activation(tmp[:, j:j + 1, :], x[:, bass.ds(n, 1), :],
                                             ACT.Square).then_inc(sq_done, 1)
                    if not stop:
                        w_split_hi(act, u + n_u + 1, (n_u - 1) % 2, split_sizes(ks, n_u - 1))
            loop_of_two(act, body, name == "ffn3")

        def loop_of_two(eng, body, last):
            if last:
                body(0, False)
                body(1, True)
            else:
                with eng.Fori(0, 2) as i:
                    body(i, False)

        def dve_residual(dve, name, u0, p0, ks, r, res, block, factor, col_n):
            n_u, in_ffn = len(ks), name[:3] == "ffn"
            sum_clear(dve, r)
            dve.wait_ge(mod_ready, block + 1)
            nc.vector.tensor_scalar(g_col[:], mod[:, block, :], factor, None, ALU.mult).then_inc(col_ready, 1)
            dve.wait_ge(col_ready, col_n)

            def body(i, last):
                for b in range(2):
                    u, p = i * (2 * n_u) + u0 + n_u * b, i * 2 + p0 + b
                    stop = last and b == 1
                    for j in range(n_u - 2 if stop else n_u - 1):
                        if not in_ffn or j % 2 == 0:
                            w_split_lo(dve, u + j + 2, j % 2, split_sizes(ks, j))
                    dve.wait_ge(unit_used, u + n_u)
                    for j in range(2):
                        n = i * 4 + 2 * b + j
                        nc.vector.scalar_tensor_tensor(
                            out=x[:, bass.ds(n, 1), :], in0=ps[:, 2 * b + j:2 * b + j + 1, :],
                            scalar=g_col[:, bass.ds(n, 1)], in1=x[:, bass.ds(n, 1), :], op0=ALU.mult,
                            op1=ALU.add).then_inc(x_first if j == 0 else pair_free, 1)
                    for j in range(2):
                        n = i * 4 + 2 * b + j
                        dve.wait_ge(sq_done, n + 8 * r + 1)
                        dve.wait_ge(sum_done, n + 9 * r + 1)
                        nc.vector.tensor_tensor(tmp[:, 2, :], tmp[:, 2, :], tmp[:, j, :],
                                                ALU.add).then_inc(sum_done, 1)
                    if not stop and not in_ffn:
                        w_split_lo(dve, u + n_u + 1, (n_u - 1) % 2, split_sizes(ks, n_u - 1))
            loop_of_two(dve, body, name == "ffn3")

        def pool_ffn(pool, f):
            u0 = UNIT0[f"ffn{f}"]
            d0 = u0 + 2 * FT
            with pool.Fori(0, FT) as i:
                w_split_lo(pool, i * 2 + u0 + 3, 1)
            n_u = len(DOWN_KS)

            def down_pair(pair, last):
                for j in range(1, n_u - 2 if last else n_u, 2):
                    w_split_lo(pool, pair * n_u + d0 + j + 2, 1, split_sizes(DOWN_KS, j))
            with pool.Fori(0, 3) as pair:
                down_pair(pair, False)
            down_pair(3, f == 3)

        def act_ffn(act, f, r_next):
            name = f"ffn{f}"
            u0, p0 = UNIT0[name], PAIR0[name]

            def body(i, last=False):
                for b in range(2):
                    u, p = i * 4 + u0 + 2 * b, i * 2 + p0 + b
                    act.wait_ge(unit_used, u + 2)
                    act.wait_ge(pair_free, p + 1)
                    nc.scalar.activation(silu_g[:, b, :], ps[:, 2 * b, :], ACT.Silu).then_inc(silu_done, 1)
                    w_split_hi(act, u + 3, 1)
                    act.wait_ge(pair_free, p + 3)
                    t = i * 2 + b
                    t = slice(t, t + 1) if isinstance(t, int) else bass.ds(t, 1)
                    nc.scalar.copy(act_hi[:, t, :], prod[:, b:b + 1, :]).then_inc(act_hi_done, 1)
                    if not (last and b == 1):
                        w_split_hi(act, u + 4, 0)

            w_split_hi(act, u0 + 2, 0)
            with act.Fori(0, FT // 2 - 1) as i:
                body(i)
            body(FT // 2 - 1, last=True)
            act_residual(act, name, u0 + 2 * FT, p0 + FT, DOWN_KS, r_next, (0, 2, 3, 5)[f])

        def dve_ffn(dve, f, r_next, block, col_n):
            name = f"ffn{f}"
            u0, p0 = UNIT0[name], PAIR0[name]
            block0, blocks = ADA_IN_FFN[f]
            if f > 0:
                dve.wait_ge(k_stored, 16 * (4 if f == 1 else 16))
                dve.wait_ge(v_stored, 16 * (4 if f == 1 else 16))
                dve.wait_ge(q_stored, 16 * (16 if f == 3 else 4))

            def body(i, with_ada, ada_before):
                for b in range(2):
                    u, p, t = i * 4 + u0 + 2 * b, i * 2 + p0 + b, i * 2 + b
                    w_split_lo(dve, u + 2, 0)
                    if with_ada:
                        ada_add(dve, i + block0, 4 * b)
                        ada_add(dve, i + block0, 4 * b + 1)
                    if ada_before and b == 0:
                        mod_store(dve, i + block0 - 1)
                    dve.wait_ge(silu_done, t + FT * f + 1)
                    nc.vector.tensor_tensor(prod[:, b, :], ps[:, 2 * b + 1, :], silu_g[:, b, :],
                                            ALU.mult).then_inc(pair_free, 1)
                    dve.wait_ge(act_hi_done, t + FT * f + 1)
                    at = slice(t, t + 1) if isinstance(t, int) else bass.ds(t, 1)
                    nc.vector.tensor_tensor(act_lo[:, at, :], prod[:, b:b + 1, :],
                                            act_hi[:, at, :].bitcast(F32),
                                            ALU.subtract).then_inc(act_lo_done, 1)
                    if with_ada:
                        ada_add(dve, i + block0, 4 * b + 2)
                        ada_add(dve, i + block0, 4 * b + 3)

            if blocks:
                body(0, True, False)
                with dve.Fori(1, blocks) as i:
                    body(i, True, True)
                body(blocks, False, True)
                with dve.Fori(blocks + 1, FT // 2) as i:
                    body(i, False, False)
            else:
                with dve.Fori(0, FT // 2) as i:
                    body(i, False, False)
            dve_residual(dve, name, u0 + 2 * FT, p0 + FT, DOWN_KS, r_next, (0, 2, 3, 5)[f], block, 0.5, col_n)

        def sp_ffn(sp, f):
            u0 = UNIT0[f"ffn{f}"]
            block0, blocks = ADA_IN_FFN[f]

            def body(i, with_ada, last=False):
                for b in range(2):
                    for kh in range(2):
                        src = down[f, 0] if last and b == 1 else gate_up[f, i * 2 + b + 1]
                        w_dma(sp, i * 4 + u0 + 2 * b + kh + 2, kh, src[:, kh * UNIT:(kh + 1) * UNIT])
                        if with_ada:
                            for k in range(4 * b + 2 * kh, 4 * b + 2 * kh + 2):
                                ada_dma(sp, i + block0, k)

            if f > 0:
                for kh in range(2):
                    w_dma(sp, u0 + kh, kh, gate_up[f, 0, :, kh * UNIT:(kh + 1) * UNIT])
            if blocks:
                with sp.Fori(0, blocks) as i:
                    body(i, True)
            with sp.Fori(blocks, FT // 2 - 1) as i:
                body(i, False)
            body(FT // 2 - 1, False, last=True)
            n_u, d0 = len(DOWN_KS), u0 + 2 * FT

            def down_units(pair, first):
                for j, kn in enumerate(DOWN_KS):
                    if j >= first:
                        w_dma(sp, pair * n_u + d0 + j, j % 2, down[f, pair, :, j * UNIT:j * UNIT + kn * PAIR])
            down_units(0, 2)
            with sp.Fori(1, 4) as pair:
                down_units(pair, 0)

        def rope_multiply(dve, bank, rope_n):
            dve.wait_ge(rope_done, rope_n)
            for n, (src, table) in enumerate(((0, cos), (1, sin), (1, cos), (0, sin))):
                op = nc.vector.tensor_tensor(tmp[:, n, :], ps[:, bank + src, :], table[:], ALU.mult)
            op.then_inc(pair_free, 1)

        def rope_store(pool, pair, rope_n, busy, busy_n, dst, dst_sem):
            pool.wait_ge(pair_free, pair + 3)
            pool.wait_ge(busy, busy_n)
            nc.gpsimd.tensor_tensor(rotated[:, 0, :], tmp[:, 0, :], tmp[:, 1, :],
                                    ALU.subtract).then_inc(rope_done, 1)
            nc.gpsimd.tensor_tensor(rotated[:, 1, :], tmp[:, 2, :], tmp[:, 3, :],
                                    ALU.add).then_inc(rope_done, 1)
            pool.wait_ge(rope_done, rope_n + 2)
            pool.sem_inc(carrier, 1)
            pool.dma_start(dst.rearrange("h p t -> p h t"), rotated[:]).then_inc(dst_sem, 16)

        def v_copy(dve, bank, n):
            dve.wait_ge(v_stored, n * 16)
            for half in range(2):
                op = nc.vector.tensor_copy(
                    v_out[:, :, 2 * half:2 * half + 2, :].rearrange("p j t d -> p t j d"),
                    ps[:, bank + half, :].rearrange("p (t j d) -> p t j d", t=2, j=4))
                if half == 0:
                    op.then_inc(v_out_done, 1)
            op.then_inc(pair_free, 1)

        def v_store(pool, pair, dst):
            pool.wait_ge(pair_free, pair + 3)
            pool.sem_inc(carrier, 1)
            pool.dma_start(dst.rearrange("j p n -> p j n"),
                           v_out[:].rearrange("p j t d -> p j (t d)")).then_inc(v_stored, 16)

        def act_kv(act):
            u0 = UNIT0["kv"]
            with act.Fori(0, G * NB) as i:
                for j in range(4):
                    w_split_hi(act, i * 4 + u0 + 2 + j, j % 2)

        def dve_kv(dve):
            u0, p0 = UNIT0["kv"], PAIR0["kv"]
            dve.wait_ge(tables_in, 16 * 3 + 32)
            with dve.Fori(0, G * NB) as i:
                w_split_lo(dve, i * 4 + u0 + 2, 0)
                w_split_lo(dve, i * 4 + u0 + 3, 1)
                dve.wait_ge(unit_used, i * 4 + u0 + 2)
                rope_multiply(dve, 0, i * 2 + rope_before("kv"))
                w_split_lo(dve, i * 4 + u0 + 4, 0)
                w_split_lo(dve, i * 4 + u0 + 5, 1)
                dve.wait_ge(unit_used, i * 4 + u0 + 4)
                v_copy(dve, 2, i + 4)

        def pool_kv(pool):
            p0 = PAIR0["kv"]
            with pool.Fori(0, G * NB) as i:
                rope_store(pool, i * 2 + p0, i * 2 + rope_before("kv"), k_stored, i * 16 + 64,
                           dram_k["B"].rearrange("g b h p t -> (g b) h p t")[i], k_stored)
                v_store(pool, i * 2 + p0 + 1, dram_v["B"].rearrange("g b j p n -> (g b) j p n")[i])

        def sp_kv(sp):
            u0 = UNIT0["kv"]
            for j in range(2):
                w_dma(sp, u0 + j, j, kv_w[j])
            load_tables(sp, "kv")
            for j in (2, 3):
                w_dma(sp, u0 + j, j % 2, kv_w[j])
            with sp.Fori(1, G * NB) as i:
                for j in range(4):
                    w_dma(sp, i * 4 + u0 + j, j % 2, kv_w[i * 4 + j])

        def load_tables(sp, name):
            sp.wait_ge(unit_used, UNIT0[name])
            sp.wait_ge(sq_done, 8 * (ROUND[name] + 1))
            order = 0 if name == "mixA" else 1
            sp.dma_start(cos[:], cos_t[order]).then_inc(tables_in, 16)
            sp.dma_start(sin[:], sin_t[order]).then_inc(tables_in, 16)
            if name == "mixA":
                sp.dma_start(m_a[:], mask_a).then_inc(tables_in, 16)
            if name == "mixB":
                sp.dma_start(m_b[:], mask_b).then_inc(tables_in, 16)

        TABLES = {"mixA": 48, "kv": 80, "mixB": 128}

        def head_load(sp, layer, a, j):
            is_a = layer == "A"
            nb = 1 if is_a else NB
            hd0 = 0 if is_a else HEADS
            sp.wait_ge(prep_lo, a * 12 + 3 * (hd0 + j))
            sp.wait_ge(k_stored, a * 16 + 16 if is_a else 16 * 16)
            for copy in range(2):
                for half in range(2):
                    row = 64 * copy + 32 * half
                    sp.dma_start(k_raw[row:row + 32, 0:nb, :],
                                 dram_k[layer][a, :, half, 32 * j:32 * j + 32, :]
                                 .rearrange("b i t -> i b t")).then_inc(k_landed, 16)
            sp.wait_ge(v_stored, a * 16 + 16 if is_a else 16 * 16)
            sp.dma_start(v_raw[:, 0:nb].rearrange("p b t d -> p b (t d)"),
                         dram_v[layer][a, :, j].rearrange("b p n -> p b n")).then_inc(v_landed, 16)
            sp.wait_ge(q_stored, a * 16 + 16 if is_a else a * 48 + 64 + 48)
            for copy in range(2):
                for half in range(2):
                    row = 64 * copy + 32 * half
                    sp.dma_start(q_raw[row:row + 32, 0:nb, :],
                                 dram_q[layer][a, :, half, 32 * j:32 * j + 32, :]
                                 .rearrange("b i t -> i b t")).then_inc(q_landed, 16)

        def mixer_bases(name):
            is_a = name[-1] == "A"
            return is_a, 1 if is_a else NB, 0 if is_a else HEADS, 0 if is_a else STEPS * G

        def sp_mixer(sp, name, weights):
            layer, u0 = name[-1], UNIT0[name]
            for j in range(2):
                w_dma(sp, u0 + j, j, weights[j])
            load_tables(sp, name)
            for j in (2, 3):
                w_dma(sp, u0 + j, j % 2, weights[j])

            def group(g, a, gemm, attend):
                def unit(j):
                    if gemm:
                        w_dma(sp, g * 6 + u0 + j, j % 2, weights[g * 6 + j])
                unit(4)
                unit(5)
                for j in range(3):
                    if attend:
                        head_load(sp, layer, a, j + 1)
                    unit(6 + j)
                unit(9)
                if gemm:
                    head_load(sp, layer, g, 0)

            group(0, None, True, False)
            with sp.Fori(1, G) as g:
                group(g, g - 1, True, True)
            group(None, G - 1, False, True)
            for j in range(28, 32):
                w_dma(sp, u0 + j, j % 2, weights[j])

        def act_mixer(act, name):
            is_a, nb, hd0, st0 = mixer_bases(name)
            u0 = UNIT0[name]

            def prep(a, j):
                n, sl = a * 4 + hd0 + j, j % 2
                act.wait_ge(k_landed, n * 64 + 64)
                nc.scalar.copy(k_hi[:, sl, 0:nb, :], k_raw[:, 0:nb, :]).then_inc(prep_hi, 1)
                act.wait_ge(q_landed, n * 64 + 64)
                nc.scalar.copy(q_st[:, sl, 0:nb, :], q_raw[:, 0:nb, :]).then_inc(prep_hi, 1)
                act.wait_ge(v_landed, n * 16 + 16)
                nc.scalar.copy(v_hi[:, sl, 0:nb].rearrange("p b t d -> p (b t d)"),
                               v_raw[:, 0:nb].rearrange("p b t d -> p (b t d)")).then_inc(prep_hi, 1)

            def exp(a, s):
                w = (s % 4 + 1 if is_a else 6) * P
                act.wait_ge(negmax_done, a * STEPS + st0 + s + 1)
                nc.scalar.activation(probs[:, s % 2, 0:w], probs[:, s % 2, 0:w], ACT.Exp,
                                     bias=negmax[:, s % 2:s % 2 + 1], scale=-1.0,
                                     accum_out=denom[:, s % 4:s % 4 + 1]).then_inc(exp_done, 1)

            def round_pt(a, s):
                w = (s % 4 + 1 if is_a else 6) * P
                act.wait_ge(t_done, a * STEPS + st0 + s + 1)
                nc.scalar.copy(pt_hi[:, 0:w], pt_ps[:, 0:w]).then_inc(pt_hi_done, 1)

            def att_copy(a, hp):
                act.wait_ge(ot_done, a * 2 + 2 * (st0 // STEPS) + hp + 1)
                nc.scalar.copy(att[:, bass.ds(a * 2 + hp, 1), :], ps[:, 6:7, :]).then_inc(att_done, 1)

            def group(g, a, gemm, attend):
                def split(j):
                    if gemm:
                        w_split_hi(act, g * 6 + u0 + j, j % 2)
                split(2)
                if attend:
                    prep(a, 0)
                split(3)
                if not attend:
                    for j in (4, 5, 6, 7):
                        split(j)
                    return
                for s in range(STEPS):
                    exp(a, s)
                    if s in (4, 8, 12):
                        split(3 + s // 4)
                    if s in (2, 6, 10):
                        prep(a, (s + 2) // 4)
                    if s == 11:
                        att_copy(a, 0)
                    if s >= 1:
                        round_pt(a, s - 1)
                round_pt(a, 15)
                split(7)
                att_copy(a, 1)

            group(0, None, True, False)
            with act.Fori(1, G) as g:
                group(g, g - 1, True, True)
            group(None, G - 1, False, True)

        def act_wo(act, name, r_next):
            view = by_class if name == "woA" else classes
            for k in range(KT):
                if k in (0, KT - 1):
                    act.wait_ge(att_done, (KT if name == "woA" else 2 * KT) + (1 if k else 0))
                nc.scalar.copy(classes(h_hi[:, k, :]), view(att[:, k, :])).then_inc(h_hi_done, 1)
            act_residual(act, name, UNIT0[name], PAIR0[name], FULL_KS, r_next, 1 if name == "woA" else 4)

        def dve_wo(dve, name, r_next, block, col_n):
            h0, view = h_count(name), by_class if name == "woA" else classes
            for k in range(KT):
                dve.wait_ge(h_hi_done, h0 + k + 1)
                nc.vector.tensor_tensor(classes(h_lo[:, k, :]), view(att[:, k, :]),
                                        classes(h_hi[:, k, :].bitcast(F32)),
                                        ALU.subtract).then_inc(h_lo_done, 1)
            dve_residual(dve, name, UNIT0[name], PAIR0[name], FULL_KS, r_next,
                         1 if name == "woA" else 4, block, 1.0, col_n)

        def dve_mixer(dve, name):
            is_a, nb, hd0, st0 = mixer_bases(name)
            u0, p0, rope0 = UNIT0[name], PAIR0[name], rope_before(name)
            dve.wait_ge(tables_in, TABLES[name])

            def negated_max(a, s):
                i = s % 4
                w = (i + 1 if is_a else 6) * P
                mask = m_a[:, (3 - i) * P:TT * P] if is_a else m_b[:, i, :]
                dve.wait_ge(s_done, a * STEPS + st0 + s + 1)
                dve.sem_inc(carrier, 1)
                nc.vector.tensor_tensor_reduce(
                    out=probs[:, s % 2, 0:w], in0=scores[:, 0:w], in1=mask, scale=-(HD ** -0.5),
                    scalar=FAR, op0=ALU.add, op1=ALU.min,
                    accum_out=negmax[:, s % 2:s % 2 + 1]).then_inc(negmax_done, 1)

            def o_scale(a, s):
                st = a * STEPS + st0 + s
                dve.wait_ge(exp_done, st + 1)
                nc.vector.reciprocal(rdenom[:, s % 2:s % 2 + 1],
                                     denom[:, s % 4:s % 4 + 1]).then_inc(rd_done, 1)
                dve.wait_ge(rd_done, st + 1)
                dve.wait_ge(pv_done, st + 1)
                j = s // 4
                nc.vector.tensor_scalar(o_rows[:, s % 4, j * HD:(j + 1) * HD], o_ps,
                                        rdenom[:, s % 2:s % 2 + 1], None, ALU.mult).then_inc(o_done, 1)

            def split_pt(a, s):
                w = (s % 4 + 1 if is_a else 6) * P
                dve.wait_ge(pt_hi_done, a * STEPS + st0 + s + 1)
                nc.vector.tensor_tensor(pt_lo[:, 0:w], pt_ps[:, 0:w], pt_hi[:, 0:w].bitcast(F32),
                                        ALU.subtract).then_inc(pt_lo_done, 1)

            def read_out(g, pair):
                dve.wait_ge(unit_used, g * 6 + u0 + 2 * pair + 2)
                if is_a and pair == 2:
                    v_copy(dve, 0, g)
                else:
                    per = 4 if is_a else 6
                    rope_multiply(dve, 2 * (pair % 2), g * per + rope0 + 2 * pair)

            def group(g, a, gemm, attend):
                def split(j):
                    if gemm:
                        w_split_lo(dve, g * 6 + u0 + j, j % 2)
                split(2)
                split(3)
                if not attend:
                    read_out(g, 0)
                    split(4)
                    split(5)
                    read_out(g, 1)
                    split(6)
                    read_out(g, 2)
                    split(7)
                    return
                for s in range(STEPS):
                    negated_max(a, s)
                    if s in (4, 8, 12):
                        split(3 + s // 4)
                    if gemm and s == 0:
                        read_out(g, 0)
                    if gemm and s == 8:
                        read_out(g, 1)
                    if s >= 2:
                        o_scale(a, s - 2)
                    if s >= 1:
                        split_pt(a, s - 1)
                o_scale(a, 14)
                split_pt(a, 15)
                o_scale(a, 15)
                if gemm:
                    read_out(g, 2)
                split(7)

            group(0, None, True, False)
            with dve.Fori(1, G) as g:
                group(g, g - 1, True, True)
            group(None, G - 1, False, True)

        def pool_mixer(pool, name):
            layer = name[-1]
            is_a, nb, hd0, st0 = mixer_bases(name)
            p0, rope0 = PAIR0[name], rope_before(name)

            def prep(a, j):
                n, sl = a * 12 + 3 * (hd0 + j), j % 2
                pool.wait_ge(prep_hi, n + 1)
                nc.gpsimd.tensor_tensor(k_lo[:, sl, 0:nb, :], k_raw[:, 0:nb, :],
                                        k_hi[:, sl, 0:nb, :].bitcast(F32), ALU.subtract).then_inc(prep_lo, 1)
                pool.wait_ge(prep_hi, n + 2)
                pool.wait_ge(prep_lo, n + 1)
                q_low = q_st[64:P, sl, 0:nb, :]
                nc.gpsimd.tensor_tensor(q_low, q_raw[64:P, 0:nb, :], q_low.bitcast(F32),
                                        ALU.subtract).then_inc(prep_lo, 1)
                pool.wait_ge(prep_hi, n + 3)
                pool.wait_ge(prep_lo, n + 2)
                nc.gpsimd.tensor_tensor(v_lo[:, sl, 0:nb].rearrange("p b t d -> p (b t d)"),
                                        v_raw[:, 0:nb].rearrange("p b t d -> p (b t d)"),
                                        v_hi[:, sl, 0:nb].rearrange("p b t d -> p (b t d)").bitcast(F32),
                                        ALU.subtract).then_inc(prep_lo, 1)

            def store(g, pair):
                p = g * 3 + p0 + pair
                if not is_a:
                    rope_store(pool, p, g * 6 + rope0 + 2 * pair, q_stored, g * 48 + 64 + 16 * pair,
                               dram_q["B"][g, pair], q_stored)
                elif pair == 0:
                    rope_store(pool, p, g * 4 + rope0, k_stored, g * 16, dram_q["A"][g, 0], q_stored)
                elif pair == 1:
                    rope_store(pool, p, g * 4 + rope0 + 2, q_stored, g * 16 + 16, dram_k["A"][g, 0],
                               k_stored)
                else:
                    v_store(pool, p, dram_v["A"][g, 0])

            def group(g, a, gemm, attend):
                if attend:
                    prep(a, 0)
                if gemm:
                    store(g, 0)
                if attend:
                    prep(a, 1)
                    prep(a, 2)
                if gemm:
                    store(g, 1)
                if attend:
                    prep(a, 3)
                if gemm:
                    store(g, 2)

            group(0, None, True, False)
            with pool.Fori(1, G) as g:
                group(g, g - 1, True, True)
            group(None, G - 1, False, True)

        block = ctx.enter_context(nc.Block())

        @block.sync
        def _(sp):
            sp.dma_start(c_in[:], c_col).then_inc(consts_in, 16)
            sp.dma_start(mod_bias[:], ada_bias).then_inc(consts_in, 16)
            sp.dma_start(gain[:], gains).then_inc(consts_in, 16)
            sp.dma_start(ident[:], ident_in).then_inc(consts_in, 16)
            for n in range(2):
                w_dma(sp, n, n, gate_up[0, 0, :, n * UNIT:(n + 1) * UNIT], first=True)
            sp.dma_start(x[:], x_t).then_inc(x_in, 16)
            for b in range(2):
                for k in range(KT):
                    ada_dma(sp, b, k, first=b == 0 and k < ADA_SLOTS)
            sp_ffn(sp, 0)
            sp_mixer(sp, "mixA", mixa_w)
            sp_ffn(sp, 1)
            sp_kv(sp)
            sp_ffn(sp, 2)
            sp_mixer(sp, "mixB", mixb_w)
            sp_ffn(sp, 3)
            for k in range(KT):
                sp.wait_ge(y_done, k + 1)
                sp.dma_start(out[k], x[:, k, :]).then_inc(out_stored, 16)
            sp.wait_ge(out_stored, 16 * KT)

        @block.scalar
        def _(act):
            act.sem_inc(att_done, 1)
            act.wait_ge(consts_in, 16 * 4)
            nc.scalar.activation(c_act[:], c_in[:], ACT.Silu).then_inc(c_ready, 1)
            w_split_hi(act, 0, 0, first=True)
            w_split_hi(act, 1, 1, first=True)
            act.wait_ge(x_in, 16)
            for n in range(KT):
                if n >= 2:
                    act.wait_ge(sum_done, n)
                nc.scalar.activation(tmp[:, n % 2, :], x[:, n, :], ACT.Square).then_inc(sq_done, 1)
            act.wait_ge(setup, 2)
            act_rms(act, 0)
            act_norm(act, "ffn0", SUB_BLOCK[0])
            act_ffn(act, 0, 1)
            act_rms(act, 1)
            act_norm(act, "mixA", SUB_BLOCK[1])
            act_mixer(act, "mixA")
            act_wo(act, "woA", 2)
            act_rms(act, 2)
            act_norm(act, "ffn1", SUB_BLOCK[2])
            act_ffn(act, 1, 3)
            act_rms(act, 3)
            act_norm(act, "kv", KV_BLOCK)
            act_kv(act)
            act_norm(act, "ffn2", SUB_BLOCK[3])
            act_ffn(act, 2, 4)
            act_rms(act, 4)
            act_norm(act, "mixB", SUB_BLOCK[4])
            act_mixer(act, "mixB")
            act_wo(act, "woB", 5)
            act_rms(act, 5)
            act_norm(act, "ffn3", SUB_BLOCK[5])
            act_ffn(act, 3, 6)
            act_rms(act, 6)

        @block.vector
        def _(dve):
            nc.vector.memset(ones[:], 1.0).then_inc(setup, 1)
            nc.vector.memset(eps[:], EPS).then_inc(setup, 1)
            nc.vector.memset(a_col[:], 0.0).then_inc(pair_free, 1)
            nc.vector.memset(g_col[:], 0.0).then_inc(pair_free, 1)
            w_split_lo(dve, 0, 0)
            w_split_lo(dve, 1, 1)
            nc.vector.memset(tmp[:, 2, :], 0.0).then_inc(sum_done, 1)
            for n in range(KT):
                dve.wait_ge(sq_done, n + 1)
                dve.wait_ge(sum_done, n + 1)
                nc.vector.tensor_tensor(tmp[:, 2, :], tmp[:, 2, :], tmp[:, n % 2, :],
                                        ALU.add).then_inc(sum_done, 1)
            dve.wait_ge(c_ready, 1)
            for b in range(2):
                for k in range(KT):
                    ada_add(dve, b, k)
                if b == 0:
                    dve_diag(dve, 0)
                mod_store(dve, b)
            col = 1
            dve.wait_ge(pair_free, 2)
            dve_norm(dve, "ffn0", 0, SUB_BLOCK[0], 0, col)
            dve_ffn(dve, 0, 1, SUB_BLOCK[0] + 2, col + 1)
            dve_diag(dve, 1)
            dve_norm(dve, "mixA", 1, SUB_BLOCK[1], 1, col + 2)
            dve_mixer(dve, "mixA")
            dve_wo(dve, "woA", 2, SUB_BLOCK[1] + 2, col + 3)
            dve_diag(dve, 2)
            dve_norm(dve, "ffn1", 2, SUB_BLOCK[2], 2, col + 4)
            dve_ffn(dve, 1, 3, SUB_BLOCK[2] + 2, col + 5)
            dve_diag(dve, 3)
            dve_norm(dve, "kv", 3, KV_BLOCK, GAIN_KV, col + 6)
            dve_kv(dve)
            dve_norm(dve, "ffn2", 3, SUB_BLOCK[3], 3, col + 7)
            dve_ffn(dve, 2, 4, SUB_BLOCK[3] + 2, col + 8)
            dve_diag(dve, 4)
            dve_norm(dve, "mixB", 4, SUB_BLOCK[4], 4, col + 9)
            dve_mixer(dve, "mixB")
            dve_wo(dve, "woB", 5, SUB_BLOCK[4] + 2, col + 10)
            dve_diag(dve, 5)
            dve_norm(dve, "ffn3", 5, SUB_BLOCK[5], 5, col + 11)
            dve_ffn(dve, 3, 6, SUB_BLOCK[5] + 2, col + 12)
            dve_diag(dve, 6)
            dve.wait_ge(rb_done, 7)
            for k in range(KT):
                nc.vector.scalar_tensor_tensor(out=x[:, k, :], in0=x[:, k, :],
                                               scalar=gain[:, GAIN_FINAL, k:k + 1], in1=rb,
                                               op0=ALU.mult, op1=ALU.mult).then_inc(y_done, 1)

        @block.gpsimd
        def _(pool):
            pool_ffn(pool, 0)
            pool_mixer(pool, "mixA")
            pool_ffn(pool, 1)
            pool_kv(pool)
            pool_ffn(pool, 2)
            pool_mixer(pool, "mixB")
            pool_ffn(pool, 3)

        @block.tensor
        def _(pe):
            pe.wait_ge(setup, 2)
            pe.wait_ge(consts_in, 16 * 4)
            pe_ada_sum(pe, 0)
            pe_stats(pe, ROUND["ffn0"])
            pe_ada_sum(pe, 1)
            pe_ffn(pe, 0)
            pe_stats(pe, ROUND["mixA"])
            pe_mixer(pe, "mixA")
            pe_wo(pe, "woA")
            pe_stats(pe, ROUND["ffn1"])
            pe_ffn(pe, 1)
            pe_stats(pe, ROUND["kv"])
            pe_kv(pe)
            pe_ffn(pe, 2)
            pe_stats(pe, ROUND["mixB"])
            pe_mixer(pe, "mixB")
            pe_wo(pe, "woB")
            pe_stats(pe, ROUND["ffn3"])
            pe_ffn(pe, 3)
            pe_stats(pe, ROUND["final"])


def class_order():
    return np.arange(S).reshape(S // 4, 4).T.reshape(-1)


def rope_tables():
    inv = (1.0 / (np.float32(10000.0) ** (np.arange(0, HD, 2, dtype=np.float32) / np.float32(HD)))).astype(np.float32)
    token = np.stack([np.arange(S), class_order()]).astype(np.float32)
    ang = np.tile(token[:, None, :] * inv[None, :, None], (1, 4, 1))
    return np.cos(ang), np.sin(ang)


def masks():
    dist_l = np.arange(P)[:, None] - np.arange(P)[None, :]
    m_a = np.zeros((P, TT * P), np.float32)
    m_a[:, 3 * P:] = np.where(dist_l >= 0, 0.0, MASKED)
    m_b = np.zeros((P, TT, 6 * P), np.float32)
    for c in range(TT):
        for kc in range(TT):
            dist = 4 * dist_l + c - kc
            m_b[:, c, kc * P:(kc + 1) * P] = np.where((dist >= 0) & (dist <= 128), 0.0, MASKED)
        m_b[:, c, 4 * P:5 * P] = np.where(dist_l >= 0, 0.0, MASKED)
        m_b[:, c, 5 * P:6 * P] = np.where((dist_l >= 0) & (dist_l % 4 == 0), 0.0, MASKED)
    return m_a, m_b


def pack_pair(w):
    k, n = w.shape
    return w.reshape(k // P, P, n).transpose(1, 0, 2).reshape(P, k // P * n)


def pack_units(pairs):
    packed = np.stack([pack_pair(w) for w in pairs])
    return packed.reshape(len(pairs), P, 2, UNIT).transpose(0, 2, 1, 3).reshape(2 * len(pairs), P, UNIT)


def rotary_columns(w):
    return w.reshape(D, 4, 2, HALF).transpose(0, 2, 1, 3).reshape(D, PAIR)


def columns(v):
    v = v.reshape(v.shape[:-1] + (KT, P))
    return np.moveaxis(v, -1, 0)


def kernel(**inputs):
    import ml_dtypes
    import concourse.bacc as bacc
    from concourse.bass_utils import run_bass_kernel_spmd

    v = {name: np.asarray(a) for name, a in inputs.items()}
    order = class_order()
    m_a, m_b = masks()
    cos_t, sin_t = rope_tables()

    ada = np.concatenate([v["ada_w"][0], v["kv_ada_w"], v["ada_w"][1]], axis=1)
    ada_bias = np.concatenate([v["ada_b"][0], v["kv_ada_b"], v["ada_b"][1]]).reshape(ADA_BLOCKS, D)
    gains = np.concatenate([v["norm_g"].reshape(6, D), v["kv_norm_g"][None], v["final_g"][None]])

    def halves(w):
        return w.reshape((4,) + w.shape[2:])

    gate, up, down = halves(v["ffn_w_gate"]), halves(v["ffn_w_up"]), halves(v["ffn_w_down"])
    gate_up = np.stack([gate.reshape(4, KT, P, FT, P), up.reshape(4, KT, P, FT, P)], axis=4)
    gate_up = gate_up.transpose(0, 3, 2, 1, 4, 5).reshape(4, FT, P, KT * PAIR)
    down = down.reshape(4, FT, P, 4, PAIR).transpose(0, 3, 2, 1, 4).reshape(4, 4, P, FT * PAIR)

    def out_pairs(w):
        return [w[:, n * PAIR:(n + 1) * PAIR] for n in range(4)]

    def group_columns(w, g):
        return w[:, g * PAIR:(g + 1) * PAIR]

    qkv = v["moba_w_qkv"][0].reshape(D, 3, D)
    pairs_a = []
    for g in range(G):
        pairs_a += [rotary_columns(group_columns(qkv[:, 0], g)), rotary_columns(group_columns(qkv[:, 1], g)),
                    group_columns(qkv[:, 2], g)]
    kv = v["kv_w"].reshape(D, NB, 2, D)
    pairs_kv = []
    for g in range(G):
        for b in range(NB):
            pairs_kv += [rotary_columns(group_columns(kv[:, b, 0], g)), group_columns(kv[:, b, 1], g)]
    dq = v["dil_w_q"][0].reshape(D, NB, D)
    pairs_b = [rotary_columns(group_columns(dq[:, b], g)) for g in range(G) for b in range(NB)]

    arrays = {
        "x_t": v["x"][0][order].T.reshape(KT, P, S).transpose(1, 0, 2),
        "c_col": columns(v["c"][0]),
        "ada": ada.reshape(KT, P, ADA_BLOCKS, ADA_W).transpose(2, 0, 1, 3),
        "ada_bias": columns(ada_bias),
        "gains": columns(gains),
        "gate_up": gate_up,
        "down": down,
        "mixa_w": pack_units(pairs_a + out_pairs(v["moba_w_o"][0])),
        "kv_w": pack_units(pairs_kv),
        "mixb_w": pack_units(pairs_b + out_pairs(v["dil_w_o"][0])),
        "cos_t": cos_t.astype(np.float32),
        "sin_t": sin_t.astype(np.float32),
        "mask_a": m_a.astype(ml_dtypes.bfloat16),
        "mask_b": m_b.astype(ml_dtypes.bfloat16),
        "ident_in": np.eye(P, dtype=np.float32),
    }
    arrays = {name: np.ascontiguousarray(a) for name, a in arrays.items()}
    nc = bacc.Bacc("TRN2", target_bir_lowering=False, num_devices=1)
    aps = [nc.dram_tensor(name, a.shape, mybir.dt.from_np(a.dtype), kind="ExternalInput").ap()
           for name, a in arrays.items()]
    out = nc.dram_tensor("out", (KT, P, S), F32, kind="ExternalOutput").ap()
    build(nc, *aps, out)
    got = run_bass_kernel_spmd(nc, [arrays], core_ids=[0]).results[0]["out"]
    y = np.empty((1, S, D), np.float32)
    y[0, order] = got.reshape(D, S).T
    return y
```

```python
from contextlib import ExitStack

import numpy as np

import concourse.bass as bass
from concourse import mybir

F32 = mybir.dt.float32
F32R = mybir.dt.float32r
BF16 = mybir.dt.bfloat16
ALU = mybir.AluOpType
ACT = mybir.ActivationFunctionType

P = 128
D = 1024
S = 512
F = 2816
HEADS = 16
HD = 64
EPS = 1e-6
KT = D // P
FT = F // P
TT = S // P
G = HEADS // 4
HALF = HD // 2
NB = 3
UNIT = 1024
PAIR = 256
DOWN_KS = (4, 4, 4, 4, 4, 2)
FULL_KS = (4, 4)
ADA_W = 1024
MASKED = -1e30
FAR = 3e38

FFN_UNITS = 2 * FT + 4 * len(DOWN_KS)
PHASES = (("ffn0", FFN_UNITS), ("mixA", 24), ("woA", 8), ("ffn1", FFN_UNITS), ("kv", 48),
          ("ffn2", FFN_UNITS), ("mixB", 24), ("woB", 8), ("ffn3", FFN_UNITS))
UNIT0, PAIR0 = {}, {}
_u = _p = 0
for _name, _n in PHASES:
    UNIT0[_name], PAIR0[_name] = _u, _p
    _u += _n
    _p += FT + 4 if _name[:3] == "ffn" else _n // 2
UNITS = _u
ADA_IN_FFN = {0: (2, 6), 1: (8, 6), 2: (14, 6), 3: (20, 0)}
ADA_SLOTS = 4
SUB_BLOCK = (0, 3, 6, 11, 14, 17)
KV_BLOCK = 9
ADA_BLOCKS = 20
GAIN_KV, GAIN_FINAL = 6, 7
ROUND = {"ffn0": 0, "mixA": 1, "ffn1": 2, "kv": 3, "mixB": 4, "ffn3": 5, "final": 6}

STEPS, EARLY, PRE = 16, 4, 6
SUBSTEPS = {step: (2 * step + 6, 2 * step + 7) for step in range(4)} | {step: (step + 10,) for step in range(4, 14)}
SPLIT_HI = {0: 3, 2: 4, 5: 5, 9: 6, 13: 7}
SPLIT_LO = {1: 3, 3: 4, 6: 5, 10: 6, 15: 7}
READ_OUT = {1: ((0, 0),), 2: ((0, 1),), 7: ((1, 0),), 8: ((1, 1),), 14: ((2, 0), (2, 1))}
NEXT_HEAD = {"mixA": ("k", "", "", ""), "mixB": ("k", "v", "", "")}


def build(nc, x_t, c_col, ada, ada_bias, gains, gate_up, down, mixa_w, kv_w, mixb_w, cos_t, sin_t,
          mask_a, mask_b, ident_in, out):
    with ExitStack() as ctx:
        def sem(name):
            return ctx.enter_context(nc.semaphore(name))

        def sb(stack, name, shape, dt=F32):
            return stack.enter_context(nc.sbuf_tensor(name, shape, dt))

        x = sb(ctx, "x", [P, KT, S])
        h_hi = sb(ctx, "h_hi", [P, KT, S], F32R)
        h_lo = sb(ctx, "h_lo", [P, KT, S], F32R)
        w_raw = sb(ctx, "w_raw", [P, 2, UNIT])
        w_hi = sb(ctx, "w_hi", [P, 2, UNIT], F32R)
        w_lo = sb(ctx, "w_lo", [P, 2, UNIT], F32R)
        tmp = sb(ctx, "tmp", [P, 5, S])
        diag = sb(ctx, "diag", [P, TT, P])
        ident = sb(ctx, "ident", [P, P])
        ones = sb(ctx, "ones", [P, P])
        mod = sb(ctx, "mod", [P, ADA_BLOCKS, KT])
        mod_bias = sb(ctx, "mod_bias", [P, ADA_BLOCKS, KT])
        gain = sb(ctx, "gain", [P, 8, KT])
        c_in = sb(ctx, "c_in", [P, KT])
        c_act = sb(ctx, "c_act", [P, KT])
        mod_sum = sb(ctx, "mod_sum", [P, KT])
        a_col = sb(ctx, "a_col", [P, KT])
        g_col = sb(ctx, "g_col", [P, KT])
        rms = sb(ctx, "rms", [P, TT])
        rinv = sb(ctx, "rinv", [P, TT])
        eps = sb(ctx, "eps", [P, 1])
        with ExitStack() as ffn_space:
            act_hi = sb(ffn_space, "act_hi", [P, FT, S], F32R)
            act_lo = sb(ffn_space, "act_lo", [P, FT, S], F32R)
            silu_g = sb(ffn_space, "silu_g", [P, 2, S])
            prod = sb(ffn_space, "prod", [P, 2, S])
            ada_raw = sb(ffn_space, "ada_raw", [P, ADA_SLOTS, ADA_W])
            ada_acc = sb(ffn_space, "ada_acc", [P, ADA_W])
        with ExitStack() as mixer_space:
            cos = sb(mixer_space, "cos", [P, S])
            sin = sb(mixer_space, "sin", [P, S])
            rotated = sb(mixer_space, "rotated", [P, 2, S])
            v_out = sb(mixer_space, "v_out", [P, 4, TT, HD])
            q_raw = sb(mixer_space, "q_raw", [P, NB, S])
            k_raw = sb(mixer_space, "k_raw", [P, NB, S])
            v_raw = sb(mixer_space, "v_raw", [P, NB, TT, HD])
            q_st = sb(mixer_space, "q_st", [P, 2, NB, S], F32R)
            k_hi = sb(mixer_space, "k_hi", [P, 2, NB, S], F32R)
            k_lo = sb(mixer_space, "k_lo", [P, 2, NB, S], F32R)
            v_st = sb(mixer_space, "v_st", [P, 2, NB, TT, 2, HD], F32R)
            probs = sb(mixer_space, "probs", [P, 2, 6 * P])
            pt_hi = sb(mixer_space, "pt_hi", [P, 2, 6 * P], F32R)
            pt_lo = sb(mixer_space, "pt_lo", [P, 2, 6 * P], F32R)
            o_rows = sb(mixer_space, "o_rows", [P, TT, 4 * HD])
            att = sb(mixer_space, "att", [P, KT, S])
            m_a = sb(mixer_space, "m_a", [P, TT * P], BF16)
            m_b = sb(mixer_space, "m_b", [P, TT, 6 * P], BF16)
            negmax = sb(mixer_space, "negmax", [P, 2])
            denom = sb(mixer_space, "denom", [P, 4])
            rdenom = sb(mixer_space, "rdenom", [P, 2])
            o_sum = sb(mixer_space, "o_sum", [P, 2, HD])

        ps = ctx.enter_context(nc.psum_tensor("ps", [P, 8, 512], F32))
        flat = ps[:].rearrange("p b n -> p (b n)")
        rb = ps[:, 4, :]
        stat = ps[:, 5, 0:TT]
        ada_ps = flat[:, 6 * 512:6 * 512 + ADA_W]
        scores = flat[:, 4 * 512:4 * 512 + 6 * P]
        pt_ps = flat[:, 6 * 512:6 * 512 + 6 * P]
        O_BANK = {"A": 5, "B": 3}
        OT_BANK = {"A": 7, "B": 3}

        def scratch(name, shape):
            return nc.dram_tensor(name, shape, F32, kind="Internal").ap()

        dram_q = {"A": scratch("qa", (G, 1, 2, P, S)), "B": scratch("qb", (G, NB, 2, P, S))}
        dram_k = {"A": scratch("ka", (G, 1, 2, P, S)), "B": scratch("kb", (G, NB, 2, P, S))}
        dram_v = {"A": scratch("va", (G, 1, 4, P, TT * HD)), "B": scratch("vb", (G, NB, 4, P, TT * HD))}

        w_landed = [sem("w_landed0"), sem("w_landed1")]
        w_hi_done = sem("w_hi_done")
        w_lo_done = [sem("w_lo_done0"), sem("w_lo_done1")]
        unit_used = sem("unit_used")
        pair_free = sem("pair_free")
        consts_in, x_in, tables_in = sem("consts_in"), sem("x_in"), sem("tables_in")
        c_ready, setup = sem("c_ready"), sem("setup")
        ada_landed = [sem(f"ada_landed{n}") for n in range(ADA_SLOTS)]
        ada_added = sem("ada_added")
        ada_summed = sem("ada_summed")
        lanes_summed = sem("lanes_summed")
        mod_ready = sem("mod_ready")
        col_ready = sem("col_ready")
        silu_done, act_hi_done, act_lo_done = sem("silu_done"), sem("act_hi_done"), sem("act_lo_done")
        x_first = sem("x_first")
        sq_done, sum_done = sem("sq_done"), sem("sum_done")
        stat_done, rms_done, rinv_done = sem("stat_done"), sem("rms_done"), sem("rinv_done")
        diag_done, rb_done = sem("diag_done"), sem("rb_done")
        xar_done, h_hi_done, h_lo_done = sem("xar_done"), sem("h_hi_done"), sem("h_lo_done")
        rope_done = sem("rope_done")
        q_stored, k_stored, v_stored = sem("q_stored"), sem("k_stored"), sem("v_stored")
        q_landed, k_landed, v_landed = sem("q_landed"), sem("k_landed"), sem("v_landed")
        prep_hi, prep_lo = sem("prep_hi"), sem("prep_lo")
        s_done, negmax_done, exp_done = sem("s_done"), sem("negmax_done"), sem("exp_done")
        t_done, pt_hi_done, pt_lo_done = sem("t_done"), sem("pt_hi_done"), sem("pt_lo_done")
        pv_done, rd_done, o_done = sem("pv_done"), sem("rd_done"), sem("o_done")
        o_sum_done = sem("o_sum_done")
        ot_done = sem("ot_done")
        att_done = sem("att_done")
        y_done, out_stored = sem("y_done"), sem("out_stored")
        carrier = sem("carrier")

        def classes(ap):
            return ap.rearrange("p (c l) -> p c l", c=4)

        def by_class(ap):
            return ap.rearrange("p (l c) -> p c l", c=4)


        def h_count(name):
            order = ("ffn0", "mixA", "woA", "ffn1", "kv", "ffn2", "mixB", "woB", "ffn3")
            return KT * order.index(name)

        def rope_before(name):
            return {"mixA": 0, "kv": 16, "mixB": 40}[name]

        def w_dma(sp, u, slot, src, first=False):
            if not first:
                sp.wait_ge(w_lo_done[slot], u - slot)
            n = src.shape[1]
            sp.dma_start(w_raw[:, slot, 0:n], src).then_inc(w_landed[slot], 16)

        def w_split_hi(act, u, slot, n=UNIT, first=False):
            act.wait_ge(w_landed[slot], u * 8 - slot * 8 + 16)
            if not first:
                act.wait_ge(unit_used, u - 1)
            nc.scalar.copy(w_hi[:, slot, 0:n], w_raw[:, slot, 0:n]).then_inc(w_hi_done, 1)

        def w_split_lo(eng, u, slot, n=UNIT):
            eng.wait_ge(w_hi_done, u + 1)
            eng.tensor_tensor(w_lo[:, slot, 0:n], w_raw[:, slot, 0:n],
                              w_hi[:, slot, 0:n].bitcast(F32), ALU.subtract).then_inc(w_lo_done[slot], 2)

        def three_passes(out_ap, l_hi, l_lo, r_hi, r_lo, start, stop, skip=False):
            nc.tensor.matmul(out_ap, l_hi, r_hi, start=start, stop=False, skip_group_check=skip)
            nc.tensor.matmul(out_ap, l_hi, r_lo, start=False, stop=False, skip_group_check=skip)
            return nc.tensor.matmul(out_ap, l_lo, r_hi, start=False, stop=stop, skip_group_check=skip)

        def pe_k_tile(bank, slot, k4, in_hi, in_lo, k, last_k):
            for j in range(2):
                cols = slice(k4 * PAIR + j * P, k4 * PAIR + (j + 1) * P)
                mm = three_passes(ps[:, bank + j, :], w_hi[:, slot, cols], w_lo[:, slot, cols],
                                  in_hi[:, k, :], in_lo[:, k, :], k == 0, k == last_k)
            return mm

        def pe_k_tile_v(bank, slot, k4, k, last_k):
            cols = slice(k4 * PAIR, (k4 + 1) * PAIR)
            for t in range(TT):
                o = ps[:, bank + t // 2, (t % 2) * PAIR:(t % 2 + 1) * PAIR]
                tokens = slice(t * P, (t + 1) * P)
                mm = three_passes(o, h_hi[:, k, tokens], h_lo[:, k, tokens],
                                  w_hi[:, slot, cols], w_lo[:, slot, cols],
                                  k == 0 and t % 2 == 0, k == last_k, skip=True)
            return mm

        def pe_stats(pe, r):
            pe.wait_ge(sum_done, 9 * (r + 1))
            for t in range(TT):
                mm = nc.tensor.matmul(stat[:, t:t + 1], tmp[:, 2, t * P:(t + 1) * P], ones[:, 0:1],
                                      start=True, stop=True)
            mm.then_inc(stat_done, 1)
            pe.wait_ge(diag_done, r + 1)
            nc.tensor.matmul(rb, ones[:], diag[:].rearrange("p t n -> p (t n)"),
                             start=True, stop=True).then_inc(rb_done, 1)

        def pe_ada_sum(pe, block):
            pe.wait_ge(ada_added, block * KT + KT)
            pe.wait_ge(mod_ready, block)
            for n in range(KT):
                cols = slice(n * P, (n + 1) * P)
                mm = nc.tensor.transpose(ada_ps[:, cols], ada_acc[:, cols], ident[:])
            mm.then_inc(ada_summed, 1)

        def pe_pair(pe, u0, pair, bank, ks, in_hi, in_lo, k_ready=None, between=None):
            last_k, k = sum(ks) - 1, 0
            for j, kn in enumerate(ks):
                pe.wait_ge(w_lo_done[j % 2], u0 + j - j % 2 + 2)
                if j == 0:
                    pe.wait_ge(pair_free, pair + 1)
                for k4 in range(kn):
                    if k_ready is not None:
                        k_ready(pe, k)
                    mm = pe_k_tile(bank, j % 2, k4, in_hi, in_lo, k, last_k)
                    k += 1
                mm.then_inc(unit_used, 1)
                if j == 0 and between is not None:
                    between()

        def pe_ffn(pe, f):
            name = f"ffn{f}"
            u0, p0, h0 = UNIT0[name], PAIR0[name], h_count(name)
            block0, blocks = ADA_IN_FFN[f]

            def h_ready(pe, k):
                pe.wait_ge(h_lo_done, h0 + k + 1)

            def body(i, ada_before):
                for b in range(2):
                    between = (lambda: pe_ada_sum(pe, i + block0 - 1)) if ada_before and b == 0 else None
                    pe_pair(pe, i * 4 + u0 + 2 * b, i * 2 + p0 + b, 2 * b, FULL_KS, h_hi, h_lo,
                            h_ready if b == 0 else None, between)

            body(0, False)
            if blocks:
                with pe.Fori(1, blocks + 1) as i:
                    body(i, True)
            with pe.Fori(blocks + 1, FT // 2) as i:
                body(i, False)

            def act_ready(pe, k):
                if k in (0, FT - 2, FT - 1):
                    pe.wait_ge(act_lo_done, FT * f + max(k + 1, FT - 2))
            pe_residual(pe, u0 + 2 * FT, p0 + FT, DOWN_KS, act_hi, act_lo, act_ready)

        def pe_residual(pe, u0, p0, ks, in_hi, in_lo, ready):
            with pe.Fori(0, 2) as i:
                for b in range(2):
                    pe_pair(pe, i * (2 * len(ks)) + u0 + len(ks) * b, i * 2 + p0 + b, 2 * b, ks,
                            in_hi, in_lo, ready if b == 0 else None)

        def pe_wo(pe, name):
            h0 = h_count(name)

            def h_ready(pe, k):
                pe.wait_ge(h_lo_done, h0 + k + 1)
            pe_residual(pe, UNIT0[name], PAIR0[name], FULL_KS, h_hi, h_lo, h_ready)

        def pe_kv(pe):
            u0, p0, h0 = UNIT0["kv"], PAIR0["kv"], h_count("kv")

            def h_ready(pe, k):
                pe.wait_ge(h_lo_done, h0 + k + 1)

            with pe.Fori(0, G * NB) as i:
                pe_pair(pe, i * 4 + u0, i * 2 + p0, 0, FULL_KS, h_hi, h_lo, h_ready)
                for j in range(2):
                    pe.wait_ge(w_lo_done[j], i * 4 + u0 + 2 + 2)
                    if j == 0:
                        pe.wait_ge(pair_free, i * 2 + p0 + 2)
                    for k4 in range(4):
                        mm = pe_k_tile_v(2, j, k4, 4 * j + k4, KT - 1)
                    mm.then_inc(unit_used, 1)

        def pe_mixer(pe, name):
            layer = name[-1]
            is_a = layer == "A"
            nb = 1 if is_a else NB
            u0, p0, h0 = UNIT0[name], PAIR0[name], h_count(name)
            st0, hd0 = (0, 0) if is_a else (STEPS * G, HEADS)

            def tiles(s):
                return s % 4 + 1 if is_a else 6

            def substep(g, n):
                pair, k = n // KT, n % KT
                unit, bank = n // 4, 2 * (pair % 2)
                if n % 4 == 0:
                    pe.wait_ge(w_lo_done[unit % 2], g * 6 + u0 + unit - unit % 2 + 2)
                if is_a:
                    if k == 0:
                        pe.wait_ge(pair_free, g * 3 + p0 + pair + (2 if pair == 0 else 1))
                    if n < KT:
                        pe.wait_ge(h_lo_done, h0 + k + 1)
                    if pair == 2:
                        mm = pe_k_tile_v(bank, unit % 2, k % 4, k, KT - 1)
                    else:
                        mm = pe_k_tile(bank, unit % 2, k % 4, h_hi, h_lo, k, KT - 1)
                else:
                    if n % 4 == 0:
                        pe.wait_ge(pair_free, g * 3 + p0 + pair + (1 if unit in (0, 2, 4) else 2))
                    for j in range(2):
                        kt = 2 * (n % 4) + j
                        cols = slice(kt * P, (kt + 1) * P)
                        if n < 4:
                            pe.wait_ge(h_lo_done, h0 + kt + 1)
                        mm = three_passes(ps[:, unit % 3, :], w_hi[:, unit % 2, cols],
                                          w_lo[:, unit % 2, cols], h_hi[:, kt, :], h_lo[:, kt, :],
                                          kt == 0, kt == KT - 1)
                if n % 4 == 3:
                    mm.then_inc(unit_used, 1)

            def score(a, s):
                sl, i = (s // 4) % 2, s % 4
                if i == 0:
                    pe.wait_ge(prep_lo, a * 12 + 3 * (hd0 + s // 4) + 3)
                if s >= 1:
                    pe.wait_ge(negmax_done, a * STEPS + st0 + s)
                tile, past = slice(i * P, (i + 1) * P), slice(0, (i + 1) * P)
                if is_a:
                    qs = [q_st[:, sl, 0, tile]]
                    keys = [(k_hi[:, sl, 0, past], k_lo[:, sl, 0, past], scores[:, past])]
                else:
                    keys = [(k_hi[:, sl, 0, :], k_lo[:, sl, 0, :], scores[:, 0:4 * P])]
                    for b in (1, 2):
                        keys.append((k_hi[:, sl, b, tile], k_lo[:, sl, b, tile],
                                     scores[:, (3 + b) * P:(4 + b) * P]))
                    qs = [q_st[:, sl, b, tile] for b in range(NB)]
                for q, (kh, kl, o) in zip(qs, keys):
                    nc.tensor.matmul(o, q, kh, start=True, stop=False)
                    mm = nc.tensor.matmul(o, q, kl, start=False, stop=True)
                mm.then_inc(s_done, 1)

            def transpose_p(a, s):
                st = a * STEPS + st0 + s
                pe.wait_ge(exp_done, st + 1)
                if s >= 1:
                    pe.wait_ge(pt_lo_done, st)
                for n in range(tiles(s)):
                    mm = nc.tensor.transpose(pt_ps[:, n * P:(n + 1) * P], probs[:, s % 2, n * P:(n + 1) * P],
                                             ident[:])
                mm.then_inc(t_done, 1)

            def weigh_v(a, s):
                sl, o_ps = (s // 4) % 2, ps[:, O_BANK[layer], 0:2 * HD]
                pe.wait_ge(pt_lo_done, a * STEPS + st0 + s + 1)
                if s >= 1:
                    pe.wait_ge(o_done, a * STEPS + st0 + s)
                if s in (0, 9):
                    pe.wait_ge(att_done, a * 2 + 2 * (st0 // STEPS) + (1 if s == 0 else 2))
                n_last = tiles(s) - 1
                for n in range(tiles(s)):
                    b, t = (0, n) if n < 4 else (n - 3, s % 4)
                    cols = slice(n * P, (n + 1) * P)
                    v_both = v_st[:, sl, b, t].rearrange("p h d -> p (h d)")
                    nc.tensor.matmul(o_ps, pt_hi[:, s % 2, cols], v_both, start=n == 0, stop=False)
                    mm = nc.tensor.matmul(o_ps, pt_lo[:, s % 2, cols], v_both, start=False, stop=n == n_last)
                mm.then_inc(pv_done, 1)

            def transpose_o(a, hp):
                pe.wait_ge(o_done, a * STEPS + st0 + (9 if hp == 0 else 16))
                pe.wait_ge(att_done, a * 2 + 2 * (st0 // STEPS) + hp + 1)
                for t in range(TT):
                    mm = nc.tensor.transpose(ps[:, OT_BANK[layer], t * P:(t + 1) * P],
                                             o_rows[:, t, hp * P:(hp + 1) * P], ident[:])
                mm.then_inc(ot_done, 1)

            def group(g, a, following):
                if a is None:
                    for n in range(24):
                        substep(g, n)
                    for n in range(EARLY):
                        substep(following, n)
                    return
                gemm = g is not None
                for n in range(EARLY, PRE):
                    if gemm:
                        substep(g, n)
                for s in range(STEPS):
                    subs = SUBSTEPS.get(s, ()) if gemm else ()
                    score(a, s)
                    if s == 11:
                        transpose_o(a, 0)
                    for n in subs[:1]:
                        substep(g, n)
                    if s >= 1:
                        transpose_p(a, s - 1)
                    for n in subs[1:]:
                        substep(g, n)
                    if s >= 2:
                        weigh_v(a, s - 2)
                early = range(EARLY) if following is not None else ()
                for n in early[:1]:
                    substep(following, n)
                transpose_p(a, 15)
                weigh_v(a, 14)
                for n in early[1:]:
                    substep(following, n)
                weigh_v(a, 15)
                transpose_o(a, 1)

            group(0, None, 1)
            with pe.Fori(1, G - 1) as g:
                group(g, g - 1, g + 1)
            group(G - 1, G - 2, None)
            group(None, G - 1, None)

        def ada_dma(sp, block, k, first=False):
            v, slot = block * KT + k, k % ADA_SLOTS
            if not first:
                sp.wait_ge(ada_added, v - ADA_SLOTS + 1)
            sp.dma_start(ada_raw[:, slot, :], ada[block, k]).then_inc(ada_landed[slot], 16)

        def ada_add(dve, block, k):
            v, slot = block * KT + k, k % ADA_SLOTS
            turn = k // ADA_SLOTS
            dve.wait_ge(ada_landed[slot], block * (16 * KT // ADA_SLOTS) + 16 * turn + 16)
            if k == 0:
                dve.wait_ge(ada_summed, block)
                nc.vector.tensor_scalar(ada_acc[:], ada_raw[:, slot, :], c_act[:, 0:1], None,
                                        ALU.mult).then_inc(ada_added, 1)
            else:
                dve.wait_ge(ada_added, v)
                nc.vector.scalar_tensor_tensor(out=ada_acc[:], in0=ada_raw[:, slot, :],
                                               scalar=c_act[:, k:k + 1], in1=ada_acc[:],
                                               op0=ALU.mult, op1=ALU.add).then_inc(ada_added, 1)

        def mod_store(dve, block):
            dve.wait_ge(ada_summed, block + 1)
            nc.vector.tensor_reduce(mod_sum[:], ada_ps.rearrange("p (n l) -> p n l", n=KT),
                                    mybir.AxisListType.X, ALU.add).then_inc(lanes_summed, 1)
            dve.wait_ge(lanes_summed, block + 1)
            at = slice(block, block + 1) if isinstance(block, int) else bass.ds(block, 1)
            nc.vector.tensor_tensor(mod[:, at, :], mod_sum[:].rearrange("p (o n) -> p o n", o=1),
                                    mod_bias[:, at, :], ALU.add).then_inc(mod_ready, 1)

        NORMS = ("ffn0", "mixA", "ffn1", "kv", "ffn2", "mixB", "ffn3")

        def sum_clear(dve, r):
            dve.wait_ge(stat_done, r)
            nc.vector.memset(tmp[:, 2, :], 0.0).then_inc(sum_done, 1)

        def act_rms(act, r):
            act.wait_ge(stat_done, r + 1)
            nc.scalar.activation(rms[:], stat, ACT.Sqrt, bias=eps[:, 0:1], scale=1.0 / D).then_inc(rms_done, 1)

        def dve_diag(dve, r):
            dve.wait_ge(rms_done, r + 1)
            nc.vector.reciprocal(rinv[:], rms[:]).then_inc(rinv_done, 1)
            dve.wait_ge(rinv_done, r + 1)
            for t in range(TT):
                op = nc.vector.tensor_scalar(diag[:, t, :], ident[:], rinv[:, t:t + 1], None, ALU.mult)
            op.then_inc(diag_done, 1)

        def dve_norm(dve, name, r, block, gain_row, col_n):
            h0, view = h_count(name), by_class if name == "mixA" else classes
            dve.wait_ge(mod_ready, block + 2)
            nc.vector.scalar_tensor_tensor(out=a_col[:], in0=mod[:, block + 1, :], scalar=1.0,
                                           in1=gain[:, gain_row, :], op0=ALU.add,
                                           op1=ALU.mult).then_inc(col_ready, 1)
            dve.wait_ge(col_ready, col_n)
            dve.wait_ge(rb_done, r + 1)
            dve.wait_ge(unit_used, UNIT0[name])
            if name == "ffn2":
                dve.wait_ge(rope_done, rope_before("mixB"))

            def low(k):
                dve.wait_ge(h_hi_done, h0 + k + 1)
                nc.vector.scalar_tensor_tensor(out=view(h_lo[:, k, :]), in0=classes(tmp[:, 3 + k % 2, :]),
                                               scalar=mod[:, block, k:k + 1],
                                               in1=view(h_hi[:, k, :].bitcast(F32)), op0=ALU.add,
                                               op1=ALU.subtract).then_inc(h_lo_done, 1)
            for k in range(KT):
                if k >= 2:
                    dve.wait_ge(h_lo_done, h0 + k - 1)
                nc.vector.scalar_tensor_tensor(out=tmp[:, 3 + k % 2, :], in0=x[:, k, :],
                                               scalar=a_col[:, k:k + 1], in1=rb, op0=ALU.mult,
                                               op1=ALU.mult).then_inc(xar_done, 1)
                if k >= 1:
                    low(k - 1)
            low(KT - 1)

        def act_norm(act, name, block):
            x0, view = KT * NORMS.index(name), by_class if name == "mixA" else classes
            for k in range(KT):
                act.wait_ge(xar_done, x0 + k + 1)
                nc.scalar.activation(view(h_hi[:, k, :]), classes(tmp[:, 3 + k % 2, :]), ACT.Identity,
                                     bias=mod[:, block, k:k + 1]).then_inc(h_hi_done, 1)

        def split_sizes(ks, j):
            return ks[(j + 2) % len(ks)] * PAIR

        def act_residual(act, name, u0, p0, ks, r, res):
            n_u = len(ks)

            def body(i, last):
                for b in range(2):
                    u, p = i * (2 * n_u) + u0 + n_u * b, i * 2 + p0 + b
                    stop = last and b == 1
                    for j in range(n_u - 2 if stop else n_u - 1):
                        w_split_hi(act, u + j + 2, j % 2, split_sizes(ks, j))
                    for j in range(2):
                        n = i * 4 + 2 * b + j
                        if j == 0:
                            act.wait_ge(x_first, i * 2 + 4 * res + b + 1)
                        else:
                            act.wait_ge(pair_free, p + 3)
                        act.wait_ge(sum_done, n + 9 * r)
                        nc.scalar.activation(tmp[:, j:j + 1, :], x[:, bass.ds(n, 1), :],
                                             ACT.Square).then_inc(sq_done, 1)
                    if not stop:
                        w_split_hi(act, u + n_u + 1, (n_u - 1) % 2, split_sizes(ks, n_u - 1))
            loop_of_two(act, body, name == "ffn3")

        def loop_of_two(eng, body, last):
            if last:
                body(0, False)
                body(1, True)
            else:
                with eng.Fori(0, 2) as i:
                    body(i, False)

        def dve_residual(dve, name, u0, p0, ks, r, res, block, factor, col_n):
            n_u, in_ffn = len(ks), name[:3] == "ffn"
            sum_clear(dve, r)
            dve.wait_ge(mod_ready, block + 1)
            nc.vector.tensor_scalar(g_col[:], mod[:, block, :], factor, None, ALU.mult).then_inc(col_ready, 1)
            dve.wait_ge(col_ready, col_n)

            def body(i, last):
                for b in range(2):
                    u, p = i * (2 * n_u) + u0 + n_u * b, i * 2 + p0 + b
                    stop = last and b == 1
                    for j in range(n_u - 2 if stop else n_u - 1):
                        if not in_ffn or j % 2 == 0:
                            w_split_lo(dve, u + j + 2, j % 2, split_sizes(ks, j))
                    dve.wait_ge(unit_used, u + n_u)
                    for j in range(2):
                        n = i * 4 + 2 * b + j
                        nc.vector.scalar_tensor_tensor(
                            out=x[:, bass.ds(n, 1), :], in0=ps[:, 2 * b + j:2 * b + j + 1, :],
                            scalar=g_col[:, bass.ds(n, 1)], in1=x[:, bass.ds(n, 1), :], op0=ALU.mult,
                            op1=ALU.add).then_inc(x_first if j == 0 else pair_free, 1)
                    for j in range(2):
                        n = i * 4 + 2 * b + j
                        dve.wait_ge(sq_done, n + 8 * r + 1)
                        dve.wait_ge(sum_done, n + 9 * r + 1)
                        nc.vector.tensor_tensor(tmp[:, 2, :], tmp[:, 2, :], tmp[:, j, :],
                                                ALU.add).then_inc(sum_done, 1)
                    if not stop and not in_ffn:
                        w_split_lo(dve, u + n_u + 1, (n_u - 1) % 2, split_sizes(ks, n_u - 1))
            loop_of_two(dve, body, name == "ffn3")

        def pool_ffn(pool, f):
            u0 = UNIT0[f"ffn{f}"]
            d0 = u0 + 2 * FT
            with pool.Fori(0, FT) as i:
                w_split_lo(pool, i * 2 + u0 + 3, 1)
            n_u = len(DOWN_KS)

            def down_pair(pair, last):
                for j in range(1, n_u - 2 if last else n_u, 2):
                    w_split_lo(pool, pair * n_u + d0 + j + 2, 1, split_sizes(DOWN_KS, j))
            with pool.Fori(0, 3) as pair:
                down_pair(pair, False)
            down_pair(3, f == 3)

        def act_ffn(act, f, r_next):
            name = f"ffn{f}"
            u0, p0 = UNIT0[name], PAIR0[name]

            def body(i, last=False):
                for b in range(2):
                    u, p = i * 4 + u0 + 2 * b, i * 2 + p0 + b
                    act.wait_ge(unit_used, u + 2)
                    act.wait_ge(pair_free, p + 1)
                    nc.scalar.activation(silu_g[:, b, :], ps[:, 2 * b, :], ACT.Silu).then_inc(silu_done, 1)
                    w_split_hi(act, u + 3, 1)
                    act.wait_ge(pair_free, p + 3)
                    t = i * 2 + b
                    t = slice(t, t + 1) if isinstance(t, int) else bass.ds(t, 1)
                    nc.scalar.copy(act_hi[:, t, :], prod[:, b:b + 1, :]).then_inc(act_hi_done, 1)
                    if not (last and b == 1):
                        w_split_hi(act, u + 4, 0)

            w_split_hi(act, u0 + 2, 0)
            with act.Fori(0, FT // 2 - 1) as i:
                body(i)
            body(FT // 2 - 1, last=True)
            act_residual(act, name, u0 + 2 * FT, p0 + FT, DOWN_KS, r_next, (0, 2, 3, 5)[f])

        def dve_ffn(dve, f, r_next, block, col_n):
            name = f"ffn{f}"
            u0, p0 = UNIT0[name], PAIR0[name]
            block0, blocks = ADA_IN_FFN[f]
            if f > 0:
                dve.wait_ge(k_stored, 16 * (4 if f == 1 else 16))
                dve.wait_ge(v_stored, 16 * (4 if f == 1 else 16))
                dve.wait_ge(q_stored, 16 * (16 if f == 3 else 4))

            def body(i, with_ada, ada_before):
                for b in range(2):
                    u, p, t = i * 4 + u0 + 2 * b, i * 2 + p0 + b, i * 2 + b
                    w_split_lo(dve, u + 2, 0)
                    if with_ada:
                        ada_add(dve, i + block0, 4 * b)
                        ada_add(dve, i + block0, 4 * b + 1)
                    if ada_before and b == 0:
                        mod_store(dve, i + block0 - 1)
                    dve.wait_ge(silu_done, t + FT * f + 1)
                    nc.vector.tensor_tensor(prod[:, b, :], ps[:, 2 * b + 1, :], silu_g[:, b, :],
                                            ALU.mult).then_inc(pair_free, 1)
                    dve.wait_ge(act_hi_done, t + FT * f + 1)
                    at = slice(t, t + 1) if isinstance(t, int) else bass.ds(t, 1)
                    nc.vector.tensor_tensor(act_lo[:, at, :], prod[:, b:b + 1, :],
                                            act_hi[:, at, :].bitcast(F32),
                                            ALU.subtract).then_inc(act_lo_done, 1)
                    if with_ada:
                        ada_add(dve, i + block0, 4 * b + 2)
                        ada_add(dve, i + block0, 4 * b + 3)

            if blocks:
                body(0, True, False)
                with dve.Fori(1, blocks) as i:
                    body(i, True, True)
                body(blocks, False, True)
                with dve.Fori(blocks + 1, FT // 2) as i:
                    body(i, False, False)
            else:
                with dve.Fori(0, FT // 2) as i:
                    body(i, False, False)
            dve_residual(dve, name, u0 + 2 * FT, p0 + FT, DOWN_KS, r_next, (0, 2, 3, 5)[f], block, 0.5, col_n)

        def sp_ffn(sp, f):
            u0 = UNIT0[f"ffn{f}"]
            block0, blocks = ADA_IN_FFN[f]

            def body(i, with_ada, last=False):
                for b in range(2):
                    for kh in range(2):
                        src = down[f, 0] if last and b == 1 else gate_up[f, i * 2 + b + 1]
                        w_dma(sp, i * 4 + u0 + 2 * b + kh + 2, kh, src[:, kh * UNIT:(kh + 1) * UNIT])
                        if with_ada:
                            for k in range(4 * b + 2 * kh, 4 * b + 2 * kh + 2):
                                ada_dma(sp, i + block0, k)

            if f > 0:
                for kh in range(2):
                    w_dma(sp, u0 + kh, kh, gate_up[f, 0, :, kh * UNIT:(kh + 1) * UNIT])
            if blocks:
                with sp.Fori(0, blocks) as i:
                    body(i, True)
            with sp.Fori(blocks, FT // 2 - 1) as i:
                body(i, False)
            body(FT // 2 - 1, False, last=True)
            n_u, d0 = len(DOWN_KS), u0 + 2 * FT

            def down_units(pair, first):
                for j, kn in enumerate(DOWN_KS):
                    if j >= first:
                        w_dma(sp, pair * n_u + d0 + j, j % 2, down[f, pair, :, j * UNIT:j * UNIT + kn * PAIR])
            down_units(0, 2)
            with sp.Fori(1, 4) as pair:
                down_units(pair, 0)

        def rope_multiply(dve, x1, x2, rope_n, halves=(0, 1)):
            if 0 in halves:
                dve.wait_ge(rope_done, rope_n)
            factors = ((x1, cos), (x2, sin), (x2, cos), (x1, sin))
            for half in halves:
                for n in (2 * half, 2 * half + 1):
                    src, table = factors[n]
                    op = nc.vector.tensor_tensor(tmp[:, n, :], ps[:, src, :], table[:], ALU.mult)
            if 1 in halves:
                op.then_inc(pair_free, 1)

        def rope_store(pool, pair, rope_n, busy, busy_n, dst, dst_sem):
            pool.wait_ge(pair_free, pair + 3)
            pool.wait_ge(busy, busy_n)
            nc.gpsimd.tensor_tensor(rotated[:, 0, :], tmp[:, 0, :], tmp[:, 1, :],
                                    ALU.subtract).then_inc(rope_done, 1)
            nc.gpsimd.tensor_tensor(rotated[:, 1, :], tmp[:, 2, :], tmp[:, 3, :],
                                    ALU.add).then_inc(rope_done, 1)
            pool.wait_ge(rope_done, rope_n + 2)
            pool.sem_inc(carrier, 1)
            pool.dma_start(dst.rearrange("h p t -> p h t"), rotated[:]).then_inc(dst_sem, 16)

        def v_copy(dve, bank, n, halves=(0, 1)):
            if 0 in halves:
                dve.wait_ge(v_stored, n * 16)
            for half in halves:
                op = nc.vector.tensor_copy(
                    v_out[:, :, 2 * half:2 * half + 2, :].rearrange("p j t d -> p t j d"),
                    ps[:, bank + half, :].rearrange("p (t j d) -> p t j d", t=2, j=4))
            if 1 in halves:
                op.then_inc(pair_free, 1)

        def v_store(pool, pair, dst):
            pool.wait_ge(pair_free, pair + 3)
            pool.sem_inc(carrier, 1)
            pool.dma_start(dst.rearrange("j p n -> p j n"),
                           v_out[:].rearrange("p j t d -> p j (t d)")).then_inc(v_stored, 16)

        def act_kv(act):
            u0 = UNIT0["kv"]
            with act.Fori(0, G * NB) as i:
                for j in range(4):
                    w_split_hi(act, i * 4 + u0 + 2 + j, j % 2)

        def dve_kv(dve):
            u0, p0 = UNIT0["kv"], PAIR0["kv"]
            dve.wait_ge(tables_in, 16 * 3 + 32)
            with dve.Fori(0, G * NB) as i:
                w_split_lo(dve, i * 4 + u0 + 2, 0)
                w_split_lo(dve, i * 4 + u0 + 3, 1)
                dve.wait_ge(unit_used, i * 4 + u0 + 2)
                rope_multiply(dve, 0, 1, i * 2 + rope_before("kv"))
                w_split_lo(dve, i * 4 + u0 + 4, 0)
                w_split_lo(dve, i * 4 + u0 + 5, 1)
                dve.wait_ge(unit_used, i * 4 + u0 + 4)
                v_copy(dve, 2, i + 4)

        def pool_kv(pool):
            p0 = PAIR0["kv"]
            with pool.Fori(0, G * NB) as i:
                rope_store(pool, i * 2 + p0, i * 2 + rope_before("kv"), k_stored, i * 16 + 64,
                           dram_k["B"].rearrange("g b h p t -> (g b) h p t")[i], k_stored)
                v_store(pool, i * 2 + p0 + 1, dram_v["B"].rearrange("g b j p n -> (g b) j p n")[i])

        def sp_kv(sp):
            u0 = UNIT0["kv"]
            for j in range(2):
                w_dma(sp, u0 + j, j, kv_w[j])
            load_tables(sp, "kv")
            for j in (2, 3):
                w_dma(sp, u0 + j, j % 2, kv_w[j])
            with sp.Fori(1, G * NB) as i:
                for j in range(4):
                    w_dma(sp, i * 4 + u0 + j, j % 2, kv_w[i * 4 + j])

        def load_tables(sp, name):
            sp.wait_ge(unit_used, UNIT0[name])
            sp.wait_ge(sq_done, 8 * (ROUND[name] + 1))
            order = 0 if name == "mixA" else 1
            sp.dma_start(cos[:], cos_t[order]).then_inc(tables_in, 16)
            sp.dma_start(sin[:], sin_t[order]).then_inc(tables_in, 16)
            if name == "mixA":
                sp.dma_start(m_a[:], mask_a).then_inc(tables_in, 16)
            if name == "mixB":
                sp.dma_start(m_b[:], mask_b).then_inc(tables_in, 16)

        TABLES = {"mixA": 48, "kv": 80, "mixB": 128}

        def load_rows(sp, raw, dram, a, j, landed):
            for copy in range(2):
                for half in range(2):
                    row = 64 * copy + 32 * half
                    sp.dma_start(raw[row:row + 32, 0:dram.shape[1], :],
                                 dram[a, :, half, 32 * j:32 * j + 32, :]
                                 .rearrange("b i t -> i b t")).then_inc(landed, 16)

        def first_head(layer, a, j):
            return layer == "A" and isinstance(a, int) and a == 0 and j == 0

        def load_k(sp, layer, a, j):
            is_a = layer == "A"
            hd0 = 0 if is_a else HEADS
            if not first_head(layer, a, j):
                sp.wait_ge(prep_lo, a * 12 + 3 * (hd0 + j) - 2)
            sp.wait_ge(k_stored, a * 16 + 16 if is_a else 16 * 16)
            load_rows(sp, k_raw, dram_k[layer], a, j, k_landed)

        def load_v(sp, layer, a, j):
            is_a = layer == "A"
            nb, hd0 = (1, 0) if is_a else (NB, HEADS)
            if not first_head(layer, a, j):
                sp.wait_ge(prep_lo, a * 12 + 3 * (hd0 + j) - 1)
            sp.wait_ge(v_stored, a * 16 + 16 if is_a else 16 * 16)
            sp.dma_start(v_raw[:, 0:nb].rearrange("p b t d -> p b (t d)"),
                         dram_v[layer][a, :, j].rearrange("b p n -> p b n")).then_inc(v_landed, 16)

        def load_q(sp, layer, a, j):
            hd0 = 0 if layer == "A" else HEADS
            if not first_head(layer, a, j):
                sp.wait_ge(prep_lo, a * 12 + 3 * (hd0 + j))
            sp.wait_ge(q_stored, a * 16 + 16 if layer == "A" else a * 48 + 64 + 48)
            load_rows(sp, q_raw, dram_q[layer], a, j, q_landed)

        def mixer_bases(name):
            is_a = name[-1] == "A"
            return is_a, 1 if is_a else NB, 0 if is_a else HEADS, 0 if is_a else STEPS * G

        def sp_mixer(sp, name, weights):
            layer, u0 = name[-1], UNIT0[name]
            for j in range(2):
                w_dma(sp, u0 + j, j, weights[j])
            load_tables(sp, name)
            for j in (2, 3):
                w_dma(sp, u0 + j, j % 2, weights[j])

            def group(g, a, gemm, attend):
                def unit(j):
                    if gemm:
                        w_dma(sp, g * 6 + u0 + j, j % 2, weights[g * 6 + j])
                early = not attend and layer == "B"
                if early:
                    load_k(sp, layer, g, 0)
                    load_v(sp, layer, g, 0)
                for j in range(3):
                    if attend:
                        load_k(sp, layer, a, j + 1)
                        load_v(sp, layer, a, j + 1)
                        load_q(sp, layer, a, j + 1)
                    if j == 0:
                        unit(4)
                        unit(5)
                    unit(6 + j)
                if gemm and not early:
                    load_k(sp, layer, g, 0)
                    load_v(sp, layer, g, 0)
                if gemm:
                    load_q(sp, layer, g, 0)
                unit(9)

            group(0, None, True, False)
            with sp.Fori(1, G) as g:
                group(g, g - 1, True, True)
            group(None, G - 1, False, True)
            for j in range(28, 32):
                w_dma(sp, u0 + j, j % 2, weights[j])

        def act_mixer(act, name):
            is_a, nb, hd0, st0 = mixer_bases(name)
            u0 = UNIT0[name]

            def prep(a, j, what):
                n, sl = a * 4 + hd0 + j, j % 2
                if what == "k":
                    act.wait_ge(k_landed, n * 64 + 64)
                    nc.scalar.copy(k_hi[:, sl, 0:nb, :], k_raw[:, 0:nb, :]).then_inc(prep_hi, 1)
                elif what == "v":
                    act.wait_ge(v_landed, n * 16 + 16)
                    if j != 1 and not first_head(name[-1], a, j):
                        act.wait_ge(pv_done, a * STEPS + st0 + 4 * (j - 1))
                    nc.scalar.copy(v_st[:, sl, 0:nb, :, 0, :].rearrange("p b t d -> p (b t) d"),
                                   v_raw[:, 0:nb].rearrange("p b t d -> p (b t) d")).then_inc(prep_hi, 1)
                else:
                    act.wait_ge(q_landed, n * 64 + 64)
                    nc.scalar.copy(q_st[:, sl, 0:nb, :], q_raw[:, 0:nb, :]).then_inc(prep_hi, 1)

            def exp(a, s):
                w = (s % 4 + 1 if is_a else 6) * P
                act.wait_ge(negmax_done, a * STEPS + st0 + s + 1)
                nc.scalar.activation(probs[:, s % 2, 0:w], probs[:, s % 2, 0:w], ACT.Exp,
                                     bias=negmax[:, s % 2:s % 2 + 1], scale=-1.0,
                                     accum_out=denom[:, s % 4:s % 4 + 1]).then_inc(exp_done, 1)

            def round_pt(a, s):
                w = (s % 4 + 1 if is_a else 6) * P
                act.wait_ge(t_done, a * STEPS + st0 + s + 1)
                nc.scalar.copy(pt_hi[:, s % 2, 0:w], pt_ps[:, 0:w]).then_inc(pt_hi_done, 1)

            def att_copy(a, hp):
                act.wait_ge(ot_done, a * 2 + 2 * (st0 // STEPS) + hp + 1)
                bank, n = OT_BANK[name[-1]], a * 2 + hp
                n = slice(n, n + 1) if isinstance(n, int) else bass.ds(n, 1)
                nc.scalar.copy(att[:, n, :], ps[:, bank:bank + 1, :]).then_inc(att_done, 1)

            def group(g, a, gemm, attend, early):
                def split(j):
                    if gemm:
                        w_split_hi(act, g * 6 + u0 + j, j % 2)
                if not attend:
                    split(2)
                    split(3)
                    if not is_a:
                        prep(g, 0, "k")
                        prep(g, 0, "v")
                    for j in range(4, 8):
                        split(j)
                    for what in "kvq" if is_a else "q":
                        prep(g, 0, what)
                    split(8)
                    return
                for s in range(STEPS):
                    if s == 11:
                        att_copy(a, 0)
                    if s >= 1:
                        round_pt(a, s - 1)
                    exp(a, s)
                    if s in SPLIT_HI:
                        split(SPLIT_HI[s])
                    if s < 12 and s % 4 < 3:
                        prep(a, s // 4 + 1, "kvq"[s % 4])
                    elif gemm and s >= 12 and NEXT_HEAD[name][s - 12]:
                        prep(g, 0, NEXT_HEAD[name][s - 12])
                round_pt(a, 15)
                if early:
                    split(8)
                if gemm:
                    for what in "vq" if is_a else "q":
                        prep(g, 0, what)
                att_copy(a, 1)

            group(0, None, True, False, True)
            with act.Fori(1, G - 1) as g:
                group(g, g - 1, True, True, True)
            group(G - 1, G - 2, True, True, False)
            group(None, G - 1, False, True, False)

        def act_wo(act, name, r_next):
            view = by_class if name == "woA" else classes
            for k in range(KT):
                if k in (0, KT - 1):
                    act.wait_ge(att_done, (KT if name == "woA" else 2 * KT) + (1 if k else 0))
                nc.scalar.copy(classes(h_hi[:, k, :]), view(att[:, k, :])).then_inc(h_hi_done, 1)
            act_residual(act, name, UNIT0[name], PAIR0[name], FULL_KS, r_next, 1 if name == "woA" else 4)

        def dve_wo(dve, name, r_next, block, col_n):
            h0, view = h_count(name), by_class if name == "woA" else classes
            for k in range(KT):
                dve.wait_ge(h_hi_done, h0 + k + 1)
                nc.vector.tensor_tensor(classes(h_lo[:, k, :]), view(att[:, k, :]),
                                        classes(h_hi[:, k, :].bitcast(F32)),
                                        ALU.subtract).then_inc(h_lo_done, 1)
            dve_residual(dve, name, UNIT0[name], PAIR0[name], FULL_KS, r_next,
                         1 if name == "woA" else 4, block, 1.0, col_n)

        def dve_mixer(dve, name):
            is_a, nb, hd0, st0 = mixer_bases(name)
            u0, p0, rope0 = UNIT0[name], PAIR0[name], rope_before(name)
            dve.wait_ge(tables_in, TABLES[name])

            def negated_max(a, s):
                i = s % 4
                w = (i + 1 if is_a else 6) * P
                mask = m_a[:, (3 - i) * P:TT * P] if is_a else m_b[:, i, :]
                dve.wait_ge(s_done, a * STEPS + st0 + s + 1)
                dve.sem_inc(carrier, 1)
                nc.vector.tensor_tensor_reduce(
                    out=probs[:, s % 2, 0:w], in0=scores[:, 0:w], in1=mask, scale=-(HD ** -0.5),
                    scalar=FAR, op0=ALU.add, op1=ALU.min,
                    accum_out=negmax[:, s % 2:s % 2 + 1]).then_inc(negmax_done, 1)

            def o_scale(a, s):
                st = a * STEPS + st0 + s
                dve.wait_ge(exp_done, st + 1)
                nc.vector.reciprocal(rdenom[:, s % 2:s % 2 + 1],
                                     denom[:, s % 4:s % 4 + 1]).then_inc(rd_done, 1)
                dve.wait_ge(pv_done, st + 1)
                parts = ps[:, O_BANK[name[-1]], 0:2 * HD].rearrange("p (h d) -> p d h", h=2)
                nc.vector.tensor_reduce(o_sum[:, s % 2, :], parts, mybir.AxisListType.X,
                                        ALU.add).then_inc(o_sum_done, 1)
                dve.wait_ge(rd_done, st + 1)
                dve.wait_ge(o_sum_done, st + 1)
                j = s // 4
                nc.vector.tensor_scalar(o_rows[:, s % 4, j * HD:(j + 1) * HD], o_sum[:, s % 2, :],
                                        rdenom[:, s % 2:s % 2 + 1], None, ALU.mult).then_inc(o_done, 1)

            def split_pt(a, s):
                w = (s % 4 + 1 if is_a else 6) * P
                dve.wait_ge(pt_hi_done, a * STEPS + st0 + s + 1)
                nc.vector.tensor_tensor(pt_lo[:, s % 2, 0:w], pt_ps[:, 0:w], pt_hi[:, s % 2, 0:w].bitcast(F32),
                                        ALU.subtract).then_inc(pt_lo_done, 1)

            def read_out(g, pair, half):
                dve.wait_ge(unit_used, g * 6 + u0 + 2 * pair + 2)
                if is_a and pair == 2:
                    v_copy(dve, 0, g, (half,))
                elif is_a:
                    rope_multiply(dve, 2 * pair, 2 * pair + 1, g * 4 + rope0 + 2 * pair, (half,))
                else:
                    rope_multiply(dve, 2 * pair % 3, (2 * pair + 1) % 3, g * 6 + rope0 + 2 * pair, (half,))

            def group(g, a, gemm, attend, early):
                def split(j):
                    if gemm:
                        w_split_lo(dve, g * 6 + u0 + j, j % 2)
                if not attend:
                    split(2)
                    split(3)
                    read_out(g, 0, 0)
                    read_out(g, 0, 1)
                    split(4)
                    split(5)
                    read_out(g, 1, 0)
                    read_out(g, 1, 1)
                    split(6)
                    split(7)
                    read_out(g, 2, 0)
                    read_out(g, 2, 1)
                    split(8)
                    return
                for s in range(STEPS):
                    negated_max(a, s)
                    if s in SPLIT_LO:
                        split(SPLIT_LO[s])
                    halves = READ_OUT.get(s, ()) if gemm else ()
                    for pair, half in halves[:1]:
                        read_out(g, pair, half)
                    if s >= 1:
                        split_pt(a, s - 1)
                    for pair, half in halves[1:]:
                        read_out(g, pair, half)
                    if s >= 2:
                        o_scale(a, s - 2)
                split_pt(a, 15)
                o_scale(a, 14)
                if early:
                    split(8)
                o_scale(a, 15)

            group(0, None, True, False, True)
            with dve.Fori(1, G - 1) as g:
                group(g, g - 1, True, True, True)
            group(G - 1, G - 2, True, True, False)
            group(None, G - 1, False, True, False)

        def pool_mixer(pool, name):
            layer = name[-1]
            is_a, nb, hd0, st0 = mixer_bases(name)
            p0, rope0 = PAIR0[name], rope_before(name)

            def prep(a, j, what):
                n, sl = a * 12 + 3 * (hd0 + j), j % 2
                if what == "k":
                    pool.wait_ge(prep_hi, n + 1)
                    nc.gpsimd.tensor_tensor(k_lo[:, sl, 0:nb, :], k_raw[:, 0:nb, :],
                                            k_hi[:, sl, 0:nb, :].bitcast(F32), ALU.subtract).then_inc(prep_lo, 1)
                elif what == "v":
                    high, low = (v_st[:, sl, 0:nb, :, part, :].rearrange("p b t d -> p (b t) d") for part in (0, 1))
                    pool.wait_ge(prep_hi, n + 2)
                    nc.gpsimd.tensor_tensor(low, v_raw[:, 0:nb].rearrange("p b t d -> p (b t) d"),
                                            high.bitcast(F32), ALU.subtract).then_inc(prep_lo, 1)
                else:
                    q_low = q_st[64:P, sl, 0:nb, :]
                    pool.wait_ge(prep_hi, n + 3)
                    pool.wait_ge(prep_lo, n + 2)
                    nc.gpsimd.tensor_tensor(q_low, q_raw[64:P, 0:nb, :], q_low.bitcast(F32),
                                            ALU.subtract).then_inc(prep_lo, 1)
                    pool.wait_ge(prep_lo, n + 3)

            def store(g, pair):
                p = g * 3 + p0 + pair
                if not is_a:
                    rope_store(pool, p, g * 6 + rope0 + 2 * pair, q_stored, g * 48 + 64 + 16 * pair,
                               dram_q["B"][g, pair], q_stored)
                elif pair == 0:
                    rope_store(pool, p, g * 4 + rope0, k_stored, g * 16, dram_q["A"][g, 0], q_stored)
                elif pair == 1:
                    rope_store(pool, p, g * 4 + rope0 + 2, q_stored, g * 16 + 16, dram_k["A"][g, 0],
                               k_stored)
                else:
                    v_store(pool, p, dram_v["A"][g, 0])

            def group(g, a, gemm, attend):
                if not attend and not is_a:
                    prep(g, 0, "k")
                    prep(g, 0, "v")
                for j in range(3):
                    if attend:
                        for what in "kvq":
                            prep(a, j + 1, what)
                    if gemm and j == 0:
                        store(g, 0)
                    if gemm and j == (1 if is_a else 2):
                        store(g, 1)
                if gemm:
                    if attend or is_a:
                        for what in "k" if is_a else "kv":
                            prep(g, 0, what)
                    store(g, 2)
                    for what in "vq" if is_a else "q":
                        prep(g, 0, what)

            group(0, None, True, False)
            with pool.Fori(1, G) as g:
                group(g, g - 1, True, True)
            group(None, G - 1, False, True)

        block = ctx.enter_context(nc.Block())

        @block.sync
        def _(sp):
            sp.dma_start(c_in[:], c_col).then_inc(consts_in, 16)
            sp.dma_start(mod_bias[:], ada_bias).then_inc(consts_in, 16)
            sp.dma_start(gain[:], gains).then_inc(consts_in, 16)
            sp.dma_start(ident[:], ident_in).then_inc(consts_in, 16)
            for n in range(2):
                w_dma(sp, n, n, gate_up[0, 0, :, n * UNIT:(n + 1) * UNIT], first=True)
            sp.dma_start(x[:], x_t).then_inc(x_in, 16)
            for b in range(2):
                for k in range(KT):
                    ada_dma(sp, b, k, first=b == 0 and k < ADA_SLOTS)
            sp_ffn(sp, 0)
            sp_mixer(sp, "mixA", mixa_w)
            sp_ffn(sp, 1)
            sp_kv(sp)
            sp_ffn(sp, 2)
            sp_mixer(sp, "mixB", mixb_w)
            sp_ffn(sp, 3)
            for k in range(KT):
                sp.wait_ge(y_done, k + 1)
                sp.dma_start(out[k], x[:, k, :]).then_inc(out_stored, 16)
            sp.wait_ge(out_stored, 16 * KT)

        @block.scalar
        def _(act):
            act.sem_inc(att_done, 1)
            act.wait_ge(consts_in, 16 * 4)
            nc.scalar.activation(c_act[:], c_in[:], ACT.Silu).then_inc(c_ready, 1)
            w_split_hi(act, 0, 0, first=True)
            w_split_hi(act, 1, 1, first=True)
            act.wait_ge(x_in, 16)
            for n in range(KT):
                if n >= 2:
                    act.wait_ge(sum_done, n)
                nc.scalar.activation(tmp[:, n % 2, :], x[:, n, :], ACT.Square).then_inc(sq_done, 1)
            act.wait_ge(setup, 2)
            act_rms(act, 0)
            act_norm(act, "ffn0", SUB_BLOCK[0])
            act_ffn(act, 0, 1)
            act_rms(act, 1)
            act_norm(act, "mixA", SUB_BLOCK[1])
            act_mixer(act, "mixA")
            act_wo(act, "woA", 2)
            act_rms(act, 2)
            act_norm(act, "ffn1", SUB_BLOCK[2])
            act_ffn(act, 1, 3)
            act_rms(act, 3)
            act_norm(act, "kv", KV_BLOCK)
            act_kv(act)
            act_norm(act, "ffn2", SUB_BLOCK[3])
            act_ffn(act, 2, 4)
            act_rms(act, 4)
            act_norm(act, "mixB", SUB_BLOCK[4])
            act_mixer(act, "mixB")
            act_wo(act, "woB", 5)
            act_rms(act, 5)
            act_norm(act, "ffn3", SUB_BLOCK[5])
            act_ffn(act, 3, 6)
            act_rms(act, 6)

        @block.vector
        def _(dve):
            nc.vector.memset(ones[:], 1.0).then_inc(setup, 1)
            nc.vector.memset(eps[:], EPS).then_inc(setup, 1)
            nc.vector.memset(a_col[:], 0.0).then_inc(pair_free, 1)
            nc.vector.memset(g_col[:], 0.0).then_inc(pair_free, 1)
            w_split_lo(dve, 0, 0)
            w_split_lo(dve, 1, 1)
            dve.wait_ge(c_ready, 1)
            for b in range(2):
                for k in range(KT):
                    ada_add(dve, b, k)
                if b == 0:
                    dve_diag(dve, 0)
                mod_store(dve, b)
            col = 1
            dve.wait_ge(pair_free, 2)
            dve_norm(dve, "ffn0", 0, SUB_BLOCK[0], 0, col)
            dve_ffn(dve, 0, 1, SUB_BLOCK[0] + 2, col + 1)
            dve_diag(dve, 1)
            dve_norm(dve, "mixA", 1, SUB_BLOCK[1], 1, col + 2)
            dve_mixer(dve, "mixA")
            dve_wo(dve, "woA", 2, SUB_BLOCK[1] + 2, col + 3)
            dve_diag(dve, 2)
            dve_norm(dve, "ffn1", 2, SUB_BLOCK[2], 2, col + 4)
            dve_ffn(dve, 1, 3, SUB_BLOCK[2] + 2, col + 5)
            dve_diag(dve, 3)
            dve_norm(dve, "kv", 3, KV_BLOCK, GAIN_KV, col + 6)
            dve_kv(dve)
            dve_norm(dve, "ffn2", 3, SUB_BLOCK[3], 3, col + 7)
            dve_ffn(dve, 2, 4, SUB_BLOCK[3] + 2, col + 8)
            dve_diag(dve, 4)
            dve_norm(dve, "mixB", 4, SUB_BLOCK[4], 4, col + 9)
            dve_mixer(dve, "mixB")
            dve_wo(dve, "woB", 5, SUB_BLOCK[4] + 2, col + 10)
            dve_diag(dve, 5)
            dve_norm(dve, "ffn3", 5, SUB_BLOCK[5], 5, col + 11)
            dve_ffn(dve, 3, 6, SUB_BLOCK[5] + 2, col + 12)
            dve_diag(dve, 6)
            dve.wait_ge(rb_done, 7)
            for k in range(KT):
                nc.vector.scalar_tensor_tensor(out=x[:, k, :], in0=x[:, k, :],
                                               scalar=gain[:, GAIN_FINAL, k:k + 1], in1=rb,
                                               op0=ALU.mult, op1=ALU.mult).then_inc(y_done, 1)

        @block.gpsimd
        def _(pool):
            nc.gpsimd.memset(tmp[:, 2, :], 0.0).then_inc(sum_done, 1)
            for n in range(KT):
                pool.wait_ge(sq_done, n + 1)
                pool.wait_ge(sum_done, n + 1)
                nc.gpsimd.tensor_tensor(tmp[:, 2, :], tmp[:, 2, :], tmp[:, n % 2, :],
                                        ALU.add).then_inc(sum_done, 1)
            pool_ffn(pool, 0)
            pool_mixer(pool, "mixA")
            pool_ffn(pool, 1)
            pool_kv(pool)
            pool_ffn(pool, 2)
            pool_mixer(pool, "mixB")
            pool_ffn(pool, 3)

        @block.tensor
        def _(pe):
            pe.wait_ge(setup, 2)
            pe.wait_ge(consts_in, 16 * 4)
            pe_ada_sum(pe, 0)
            pe_stats(pe, ROUND["ffn0"])
            pe_ada_sum(pe, 1)
            pe_ffn(pe, 0)
            pe_stats(pe, ROUND["mixA"])
            pe_mixer(pe, "mixA")
            pe_wo(pe, "woA")
            pe_stats(pe, ROUND["ffn1"])
            pe_ffn(pe, 1)
            pe_stats(pe, ROUND["kv"])
            pe_kv(pe)
            pe_ffn(pe, 2)
            pe_stats(pe, ROUND["mixB"])
            pe_mixer(pe, "mixB")
            pe_wo(pe, "woB")
            pe_stats(pe, ROUND["ffn3"])
            pe_ffn(pe, 3)
            pe_stats(pe, ROUND["final"])


def class_order():
    return np.arange(S).reshape(S // 4, 4).T.reshape(-1)


def rope_tables():
    inv = (1.0 / (np.float32(10000.0) ** (np.arange(0, HD, 2, dtype=np.float32) / np.float32(HD)))).astype(np.float32)
    token = np.stack([np.arange(S), class_order()]).astype(np.float32)
    ang = np.tile(token[:, None, :] * inv[None, :, None], (1, 4, 1))
    return np.cos(ang), np.sin(ang)


def masks():
    dist_l = np.arange(P)[:, None] - np.arange(P)[None, :]
    m_a = np.zeros((P, TT * P), np.float32)
    m_a[:, 3 * P:] = np.where(dist_l >= 0, 0.0, MASKED)
    m_b = np.zeros((P, TT, 6 * P), np.float32)
    for c in range(TT):
        for kc in range(TT):
            dist = 4 * dist_l + c - kc
            m_b[:, c, kc * P:(kc + 1) * P] = np.where((dist >= 0) & (dist <= 128), 0.0, MASKED)
        m_b[:, c, 4 * P:5 * P] = np.where(dist_l >= 0, 0.0, MASKED)
        m_b[:, c, 5 * P:6 * P] = np.where((dist_l >= 0) & (dist_l % 4 == 0), 0.0, MASKED)
    return m_a, m_b


def pack_pair(w):
    k, n = w.shape
    return w.reshape(k // P, P, n).transpose(1, 0, 2).reshape(P, k // P * n)


def pack_units(pairs):
    packed = np.stack([pack_pair(w) for w in pairs])
    return packed.reshape(len(pairs), P, 2, UNIT).transpose(0, 2, 1, 3).reshape(2 * len(pairs), P, UNIT)


def pack_tiles(pairs):
    return np.stack([pack_pair(w[:, j * P:(j + 1) * P]) for w in pairs for j in range(2)])


def rotary_columns(w):
    return w.reshape(D, 4, 2, HALF).transpose(0, 2, 1, 3).reshape(D, PAIR)


def columns(v):
    v = v.reshape(v.shape[:-1] + (KT, P))
    return np.moveaxis(v, -1, 0)


def kernel(**inputs):
    import ml_dtypes
    import concourse.bacc as bacc
    from concourse.bass_utils import run_bass_kernel_spmd

    v = {name: np.asarray(a) for name, a in inputs.items()}
    order = class_order()
    m_a, m_b = masks()
    cos_t, sin_t = rope_tables()

    ada = np.concatenate([v["ada_w"][0], v["kv_ada_w"], v["ada_w"][1]], axis=1)
    ada_bias = np.concatenate([v["ada_b"][0], v["kv_ada_b"], v["ada_b"][1]]).reshape(ADA_BLOCKS, D)
    gains = np.concatenate([v["norm_g"].reshape(6, D), v["kv_norm_g"][None], v["final_g"][None]])

    def halves(w):
        return w.reshape((4,) + w.shape[2:])

    gate, up, down = halves(v["ffn_w_gate"]), halves(v["ffn_w_up"]), halves(v["ffn_w_down"])
    gate_up = np.stack([gate.reshape(4, KT, P, FT, P), up.reshape(4, KT, P, FT, P)], axis=4)
    gate_up = gate_up.transpose(0, 3, 2, 1, 4, 5).reshape(4, FT, P, KT * PAIR)
    down = down.reshape(4, FT, P, 4, PAIR).transpose(0, 3, 2, 1, 4).reshape(4, 4, P, FT * PAIR)

    def out_pairs(w):
        return [w[:, n * PAIR:(n + 1) * PAIR] for n in range(4)]

    def group_columns(w, g):
        return w[:, g * PAIR:(g + 1) * PAIR]

    qkv = v["moba_w_qkv"][0].reshape(D, 3, D)
    pairs_a = []
    for g in range(G):
        pairs_a += [rotary_columns(group_columns(qkv[:, 0], g)), rotary_columns(group_columns(qkv[:, 1], g)),
                    group_columns(qkv[:, 2], g)]
    kv = v["kv_w"].reshape(D, NB, 2, D)
    pairs_kv = []
    for g in range(G):
        for b in range(NB):
            pairs_kv += [rotary_columns(group_columns(kv[:, b, 0], g)), group_columns(kv[:, b, 1], g)]
    dq = v["dil_w_q"][0].reshape(D, NB, D)
    pairs_b = [rotary_columns(group_columns(dq[:, b], g)) for g in range(G) for b in range(NB)]

    arrays = {
        "x_t": v["x"][0][order].T.reshape(KT, P, S).transpose(1, 0, 2),
        "c_col": columns(v["c"][0]),
        "ada": ada.reshape(KT, P, ADA_BLOCKS, ADA_W).transpose(2, 0, 1, 3),
        "ada_bias": columns(ada_bias),
        "gains": columns(gains),
        "gate_up": gate_up,
        "down": down,
        "mixa_w": pack_units(pairs_a + out_pairs(v["moba_w_o"][0])),
        "kv_w": pack_units(pairs_kv),
        "mixb_w": np.concatenate([pack_tiles(pairs_b), pack_units(out_pairs(v["dil_w_o"][0]))]),
        "cos_t": cos_t.astype(np.float32),
        "sin_t": sin_t.astype(np.float32),
        "mask_a": m_a.astype(ml_dtypes.bfloat16),
        "mask_b": m_b.astype(ml_dtypes.bfloat16),
        "ident_in": np.eye(P, dtype=np.float32),
    }
    arrays = {name: np.ascontiguousarray(a) for name, a in arrays.items()}
    nc = bacc.Bacc("TRN2", target_bir_lowering=False, num_devices=1)
    aps = [nc.dram_tensor(name, a.shape, mybir.dt.from_np(a.dtype), kind="ExternalInput").ap()
           for name, a in arrays.items()]
    out = nc.dram_tensor("out", (KT, P, S), F32, kind="ExternalOutput").ap()
    build(nc, *aps, out)
    got = run_bass_kernel_spmd(nc, [arrays], core_ids=[0]).results[0]["out"]
    y = np.empty((1, S, D), np.float32)
    y[0, order] = got.reshape(D, S).T
    return y
```
